# Optimizing a Trainium2 kernel written in Bass

```python
import jax, jax.numpy as jnp
from jax import lax
import numpy as np

D_MODEL = 1024
BATCH = 1
SEQ = 1024
DEPTH = 1

CHUNK = 64
N_MEM = 256
EPS = 1e-6
NEG = -1e30

A_HEADS = 8
A_KV_HEADS = 2
A_HEAD_DIM = 64
A_WINDOW = 128
A_WIN_CHUNKS = A_WINDOW // CHUNK
A_WIDTH = A_HEADS * A_HEAD_DIM

B_HEADS = 4
B_QK_DIM = 64
B_V_DIM = 2 * B_QK_DIM
B_WIDTH = B_HEADS * B_V_DIM
B_QBLOCK = 128

M_HEADS = 4
M_HEAD_DIM = 128
M_WIDTH = M_HEADS * M_HEAD_DIM

MIX_WIDTH = A_WIDTH + B_WIDTH + M_WIDTH

IN_SIZES = [
    A_WIDTH,
    A_KV_HEADS * A_HEAD_DIM,
    A_KV_HEADS * A_HEAD_DIM,
    A_WIDTH,
    2 * B_HEADS * B_QK_DIM,
    2 * B_HEADS * B_QK_DIM,
    B_WIDTH,
    B_WIDTH,
    M_WIDTH,
    M_WIDTH,
]
IN_COLS = int(sum(IN_SIZES))
IN_SPLITS = [int(v) for v in np.cumsum(IN_SIZES)[:-1]]

kernel_name = "hybrid_swa_sink_diffattn_memxattn_block"

def alibi_slopes(n):
    return jnp.asarray(np.array([2.0 ** (-8.0 * (i + 1) / n) for i in range(n)], dtype=np.float32))

def lambda_init_fn(layer_idx):
    return 0.8 - 0.6 * float(np.exp(-0.3 * layer_idx))

def rmsnorm(x, g):
    xf = x.astype(jnp.float32)
    xf = xf * lax.rsqrt(jnp.mean(xf * xf, axis=-1, keepdims=True) + EPS)
    return (xf * g.astype(jnp.float32)).astype(x.dtype)

def swa_sink_attention(q, k, v, sinks, slopes):
    b, s, h, d = q.shape
    nc = s // CHUNK
    g = h // A_KV_HEADS
    band = A_WIN_CHUNKS * CHUNK
    qc = q.reshape(b, nc, CHUNK, A_KV_HEADS, g, d)
    kc = k.reshape(b, nc, CHUNK, A_KV_HEADS, d)
    vc = v.reshape(b, nc, CHUNK, A_KV_HEADS, d)

    def shift(t, j):
        if j == 0:
            return t
        return jnp.pad(t, ((0, 0), (j, 0), (0, 0), (0, 0), (0, 0)))[:, :nc]

    kb = jnp.concatenate([shift(kc, j) for j in reversed(range(A_WIN_CHUNKS))], axis=2)
    vb = jnp.concatenate([shift(vc, j) for j in reversed(range(A_WIN_CHUNKS))], axis=2)

    logits = jnp.einsum('bnqkgd,bnskd->bnkgqs', qc, kb).astype(jnp.float32) * (d ** -0.5)
    qpos = jnp.arange(CHUNK) + (A_WIN_CHUNKS - 1) * CHUNK
    kpos = jnp.arange(band)
    dist = jnp.abs(qpos[:, None] - kpos[None, :]).astype(jnp.float32)
    sl = slopes.reshape(A_KV_HEADS, g)
    logits = logits - sl[None, None, :, :, None, None] * dist
    key_chunk = jnp.arange(nc)[:, None] - (A_WIN_CHUNKS - 1) + kpos[None, :] // CHUNK
    valid = key_chunk >= 0
    logits = jnp.where(valid[None, :, None, None, None, :], logits, NEG)
    sink = sinks.astype(jnp.float32).reshape(A_KV_HEADS, g)[None, None, :, :, None, None]
    m = jnp.maximum(jnp.max(logits, axis=-1, keepdims=True), sink)
    p = jnp.exp(logits - m)
    probs = p / (jnp.sum(p, axis=-1, keepdims=True) + jnp.exp(sink - m))
    out = jnp.einsum('bnkgqs,bnskd->bnqkgd', probs.astype(v.dtype), vb)
    return out.reshape(b, s, h * d)

def diff_attention(q, k, v, lam, slopes):
    b, s, _, h, dk = q.shape
    dv = v.shape[-1]
    nb = s // B_QBLOCK
    scale = dk ** -0.5
    qblocks = jnp.moveaxis(q.reshape(b, nb, B_QBLOCK, 2, h, dk), 1, 0)
    starts = jnp.arange(nb) * B_QBLOCK
    kpos = jnp.arange(s)

    def block(args):
        qb, start = args
        qpos = start + jnp.arange(B_QBLOCK)
        logits = jnp.einsum('bqchd,bschd->bchqs', qb, k).astype(jnp.float32) * scale
        dist = jnp.abs(qpos[:, None] - kpos[None, :]).astype(jnp.float32)
        allowed = (kpos[None, :] // CHUNK) <= (qpos[:, None] // CHUNK)
        logits = logits - slopes[None, None, :, None, None] * dist
        logits = jnp.where(allowed, logits, NEG)
        p = jax.nn.softmax(logits, axis=-1)
        attn = p[:, 0] - lam * p[:, 1]
        return jnp.einsum('bhqs,bshd->bqhd', attn.astype(v.dtype), v)

    out = lax.map(block, (qblocks, starts))
    return jnp.moveaxis(out, 0, 1).reshape(b, s, h, dv)

def memory_attention(q, memn, w_kv):
    b, s, h, d = q.shape
    kv = (memn @ w_kv).reshape(b, memn.shape[1], 2, M_HEADS, M_HEAD_DIM)
    mk, mv = kv[:, :, 0], kv[:, :, 1]
    logits = jnp.einsum('bshd,bmhd->bhsm', q, mk).astype(jnp.float32) * (d ** -0.5)
    p = jax.nn.softmax(logits, axis=-1)
    out = jnp.einsum('bhsm,bmhd->bshd', p.astype(mv.dtype), mv)
    return out.reshape(b, s, h * d)

def setup_inputs(seed: int = 0) -> dict:
    key = jax.random.key(seed)
    ks = jax.random.split(key, 16)
    f32 = jnp.float32
    x = jax.random.normal(ks[0], (BATCH, SEQ, D_MODEL), f32)
    mem = jax.random.normal(ks[1], (BATCH, N_MEM, D_MODEL), f32)
    w_in = jax.random.normal(ks[2], (DEPTH, D_MODEL, IN_COLS), f32) * D_MODEL ** -0.5
    g_norm = 1.0 + 0.02 * jax.random.normal(ks[3], (DEPTH, D_MODEL), f32)
    a_sinks = 0.5 * jax.random.normal(ks[4], (DEPTH, A_HEADS), f32)
    b_lambda_q1 = 0.1 * jax.random.normal(ks[5], (DEPTH, B_QK_DIM), f32)
    b_lambda_k1 = 0.1 * jax.random.normal(ks[6], (DEPTH, B_QK_DIM), f32)
    b_lambda_q2 = 0.1 * jax.random.normal(ks[7], (DEPTH, B_QK_DIM), f32)
    b_lambda_k2 = 0.1 * jax.random.normal(ks[8], (DEPTH, B_QK_DIM), f32)
    b_subln_g = 1.0 + 0.02 * jax.random.normal(ks[9], (DEPTH, B_V_DIM), f32)
    g_mem = 1.0 + 0.02 * jax.random.normal(ks[10], (DEPTH, D_MODEL), f32)
    w_mem_kv = jax.random.normal(ks[11], (DEPTH, D_MODEL, 2 * M_WIDTH), f32) * D_MODEL ** -0.5
    w_out = jax.random.normal(ks[12], (DEPTH, MIX_WIDTH, D_MODEL), f32) * MIX_WIDTH ** -0.5
    g_final = 1.0 + 0.02 * jax.random.normal(ks[13], (D_MODEL,), f32)
    return {"x": x, "mem": mem, "w_in": w_in, "g_norm": g_norm, "a_sinks": a_sinks,
            "b_lambda_q1": b_lambda_q1, "b_lambda_k1": b_lambda_k1,
            "b_lambda_q2": b_lambda_q2, "b_lambda_k2": b_lambda_k2,
            "b_subln_g": b_subln_g, "g_mem": g_mem, "w_mem_kv": w_mem_kv,
            "w_out": w_out, "g_final": g_final}

def reference(x, mem, w_in, g_norm, a_sinks, b_lambda_q1, b_lambda_k1, b_lambda_q2,
              b_lambda_k2, b_subln_g, g_mem, w_mem_kv, w_out, g_final):
    b, s, _ = x.shape
    a_slopes = alibi_slopes(A_HEADS)
    b_slopes = alibi_slopes(B_HEADS)
    h = x
    for l in range(DEPTH):
        hn = rmsnorm(h, g_norm[l])
        proj = hn @ w_in[l]
        aq, ak, av, ag, bq, bk, bv, bg, mq, mg = jnp.split(proj, IN_SPLITS, axis=-1)

        a_out = swa_sink_attention(aq.reshape(b, s, A_HEADS, A_HEAD_DIM),
                                   ak.reshape(b, s, A_KV_HEADS, A_HEAD_DIM),
                                   av.reshape(b, s, A_KV_HEADS, A_HEAD_DIM),
                                   a_sinks[l], a_slopes)

        lam_init = lambda_init_fn(l)
        lam = (jnp.exp(jnp.sum(b_lambda_q1[l].astype(jnp.float32) * b_lambda_k1[l].astype(jnp.float32)))
               - jnp.exp(jnp.sum(b_lambda_q2[l].astype(jnp.float32) * b_lambda_k2[l].astype(jnp.float32)))
               + lam_init)
        b_heads = diff_attention(bq.reshape(b, s, 2, B_HEADS, B_QK_DIM),
                                 bk.reshape(b, s, 2, B_HEADS, B_QK_DIM),
                                 bv.reshape(b, s, B_HEADS, B_V_DIM), lam, b_slopes)
        b_out = (rmsnorm(b_heads, b_subln_g[l]) * (1.0 - lam_init)).reshape(b, s, B_WIDTH)

        memn = rmsnorm(mem, g_mem[l])
        m_out = memory_attention(mq.reshape(b, s, M_HEADS, M_HEAD_DIM), memn, w_mem_kv[l])

        gated = jnp.concatenate([a_out * jax.nn.silu(ag),
                                 b_out * jax.nn.silu(bg),
                                 m_out * jax.nn.silu(mg)], axis=-1)
        h = h + gated @ w_out[l]
    return rmsnorm(h, g_final)


_drawn_inputs = setup_inputs


def setup_inputs(seed=0):
    import zlib

    import numpy as np

    out = dict(_drawn_inputs(seed))
    spreads = {}
    factors = {'g_norm': 5.28,
     'a_sinks': 8.0,
     'b_lambda_q1': 8.0,
     'b_lambda_q2': 3.511,
     'b_lambda_k2': 5.393,
     'b_subln_g': 8.0,
     'g_mem': 8.0,
     'g_final': 2.741}
    for name, (base, spread) in spreads.items():
        noise = np.random.default_rng([zlib.crc32(name.encode()), seed]).standard_normal(out[name].shape)
        drawn = base * np.exp(spread * noise) if base else spread * noise
        out[name] = __import__('jax').numpy.asarray(drawn.astype(out[name].dtype))
    for name, factor in factors.items():
        out[name] = (out[name] * factor).astype(out[name].dtype)
    return out
```

```python
import concourse.bass as bass
from concourse import mybir
from contextlib import ExitStack
from math import prod

F32 = mybir.dt.float32
F32R = mybir.dt.float32r
ALU = mybir.AluOpType
ACT = mybir.ActivationFunctionType
AX = mybir.AxisListType

P = 128
SEQ, D, MEM = 1024, 1024, 256
KT = D // P
ST = SEQ // P
HALF = 512
EPS = 1e-6
CHUNK = 64
HEADS = 4
DK = 64
AQ, AK, AV, AG, BQ, BK, BV, BG, MQ, MG = 0, 512, 640, 768, 1280, 1792, 2304, 2816, 3328, 3840
MIX_TILES = 12
LAM_INIT = 0.8 - 0.6
QK_SCALE = DK ** -0.5
M_SCALE = float(P) ** -0.5
MASKED = -1e30 * 2.0 ** 8

TILES = [("bk", BK, True), ("bq", BQ, True), ("bv", BV, False), ("aq", AQ, True),
         ("ag", AG, True), ("mq", MQ, False), ("mg", MG, False), ("bg", BG, False)]
NT = len(TILES)
PRE_TILES = 10
PRE_ACC = 12
PRE_T = 26

BETWEEN = {
    (2, 0, 1): [("b_scores", 0)],
    (2, 0, 2): [("b_combine", 0)],
    (2, 0, 3): [("b_scores", 1), ("b_combine", 1)],
    (3, 0, 1): [("b_spread", 0, 0), ("b_scores", 2)],
    (3, 0, 2): [("b_scores", 3)],
    (3, 0, 3): [("b_combine", 2), ("v_spread", 0)],
    (3, 1, 0): [("b_combine", 3)],
    (3, 1, 1): [("v_spread", 1)],
    (3, 1, 3): [("b_mix", 0, 0), ("b_spread", 1, 0), ("b_spread", 1, 1)],
    (4, 0, 0): [("b_scores", 4), ("b_mix", 1, 0), ("b_scores", 5), ("b_combine", 4)],
    (4, 0, 1): [("a_scores", 0)],
    (4, 0, 2): [("b_combine", 5), ("a_norm", 0)],
    (4, 1, 0): [("b_mix", 1, 1)],
    (4, 1, 1): [("b_spread", 2, 0), ("b_spread", 2, 1), ("a_scores", 1), ("a_spread", 0), ("b_spread", 2, 2)],
    (4, 1, 3): [("b_mix", 2, 0)],
    (5, 0, 0): [("b_mix", 2, 1), ("b_scores", 6), ("a_norm", 1)],
    (5, 0, 1): [("b_mix", 2, 2), ("b_scores", 7)],
    (5, 0, 2): [("b_combine", 6)],
    (5, 0, 3): [("a_scores", 2)],
    (5, 1, 1): [("b_combine", 7), ("a_norm", 2)],
    (5, 1, 2): [("a_spread", 1), ("a_mix", 0)],
    (6, 0, 0): [("b_spread", 3, 0), ("a_scores", 3)],
    (6, 0, 1): [("a_mix", 1), ("m_scores", 0), ("b_spread", 3, 1), ("m_norm", 0), ("b_spread", 3, 2)],
    (6, 0, 2): [("b_mix", 3, 0)],
    (6, 0, 3): [("b_spread", 3, 3), ("b_mix", 3, 1), ("b_mix", 3, 2)],
    (6, 1, 0): [("m_scores", 1), ("b_mix", 3, 3), ("b_squares", 0), ("m_spread", 0)],
    (6, 1, 1): [("a_spread", 2), ("m_norm", 1), ("m_mix", 0), ("m_scores", 2), ("a_norm", 3)],
    (6, 1, 2): [("b_finish", 0), ("m_spread", 1), ("m_norm", 2)],
    (7, 0, 0): [("m_scores", 3)],
    (7, 0, 1): [("a_mix", 2)],
    (7, 0, 2): [("m_spread", 2), ("m_norm", 3), ("m_mix", 1), ("a_spread", 3)],
    (7, 0, 3): [("m_mix", 2), ("m_spread", 3)],
    (7, 1, 0): [("a_mix", 3)],
    (7, 1, 1): [("b_squares", 1)],
    (7, 1, 2): [("m_mix", 3), ("b_finish", 1)],
    (7, 1, 3): [("b_gate",)],
}


def head_steps():
    out = [("start",)]
    for w in range(NT):
        out.append(("weights", w + 1))
        for s in range(2):
            for q in range(4):
                out.append(("project", w, s, q))
                if q == 3:
                    out.append(("evacuate", w, s))
                out += BETWEEN.get((w, s, q), [])
    return out


HEAD = head_steps()


def b_pieces(i):
    width = 2 * P * (i // 2 + 1)
    return [(a, min(HALF, width - a)) for a in range(0, width, HALF)]


def numbered(*events):
    return {key: n for n, key in enumerate(events)}


def score_units():
    out = []
    for s in HEAD:
        if s[0] == "b_scores":
            out += [("b", s[1], p, c) for p in range(len(b_pieces(s[1]))) for c in range(2)]
        if s[0] in ("m_scores",):
            out.append(("m", s[1]))
        if s[0] == "a_scores":
            out += [("a", s[1], g) for g in range(2)]
    return out


S_UNITS = score_units()
S_AT = numbered(*S_UNITS)
S_BY_DVE = numbered(*[u for u in S_UNITS if u[0] != "m"])
S_BY_ACT = numbered(*[u for u in S_UNITS if u[0] == "m"])
T_AT = numbered(*[s for s in HEAD if s[0] in ("v_spread", "b_spread", "m_spread", "a_spread", "b_squares")])
T_SPLIT = numbered(*[s for s in HEAD if s[0] in ("v_spread", "b_spread", "m_spread")])
PT_AT = numbered(*[s for s in HEAD if s[0] in ("b_spread", "m_spread", "b_squares")])
PT_MIX = numbered(*[s for s in HEAD if s[0] in ("b_spread", "m_spread")])
assert list(PT_MIX) == [(s[0][0] + "_spread",) + s[1:] for s in HEAD if s[0] in ("b_mix", "m_mix")]
O_AT = numbered(*[s[:2] for s in HEAD
                  if s[0] in ("m_mix", "a_mix") or (s[0] == "b_mix" and s[2] == s[1])])
NS, NTB, NPT, NO = len(S_AT), len(T_AT), len(PT_AT), len(O_AT)
S_RING, T_RING, PT_RING = 3, 2, 2
assert NS % S_RING == 0 and NTB % T_RING == 0 and NPT % PT_RING == 0 and PRE_T % T_RING == 0
NMIX = len(PT_MIX)


def build(nc, x, mem, w_in, g_norm, a_sinks, lq1, lk1, lq2, lk2, subln_g, g_mem, w_mem_kv, w_out,
          g_final, y):
    mixed = nc.dram_tensor("mixed", (MIX_TILES * P, SEQ), F32).ap()

    x_rows = x.rearrange("b (t p) d -> p (b t) d", p=P)
    y_rows = y.rearrange("b (t p) d -> p (b t) d", p=P)
    mem_rows = mem.rearrange("b (t p) d -> p (b t) d", p=P)
    w_in_v = w_in.rearrange("l (k p) n -> p (l k) n", p=P)
    w_mem_v = w_mem_kv.rearrange("l (k p) n -> p (l k) n", p=P)
    w_out_v = w_out.rearrange("l m n -> (l m) n")
    mixed_v = mixed.rearrange("(j p) s -> p j s", p=P)

    place = [(nc.sbuf_base + 63) // 64 * 64]

    def sb(name, shape, dt=F32):
        t = nc.alloc_sbuf_tensor_at(name, shape, dt, offset=place[0])
        place[0] += (prod(shape[1:]) * 4 + 31) // 32 * 32
        return t

    ctx = ExitStack()
    with ctx:
        def sem(name):
            return ctx.enter_context(nc.semaphore(name))

        w_raw = sb("w_raw", [P, 2, KT * P])
        w_hi = sb("w_hi", [P, 2, KT * P], F32R)
        w_lo = sb("w_lo", [P, 2, KT * P], F32R)
        gates = {g: sb(f"gate_{g}", [P, SEQ]) for g in "abm"}
        ident = sb("ident", [P, P])
        ones = sb("ones", [P, P], F32R)
        small = sb("small", [P, 64])
        eps = small[:, 0:1]
        neg_lam = small[:, 1:2]
        subln = small[:, 2:3]
        lam_sums = small[:, 4:6]
        lam_exps = small[:, 6:8]
        ssq = small[:, 8:10]
        std = small[:, 10:12]
        rstd = small[:, 12:14]
        sink_in = small[:, 16:24]
        sinks = small[:, 24:40]
        stats_b = sb("stats_b", [P, 32])
        b_max = stats_b[:, 0:4]
        b_neg = stats_b[:, 4:8]
        b_sum = stats_b[:, 8:12]
        b_inv = stats_b[:, 12:16]
        stats_m = sb("stats_m", [P, 8])
        m_max, m_neg, m_sum, m_inv = (stats_m[:, 2 * n:2 * n + 2] for n in range(4))
        stats_a = sb("stats_a", [P, 32])
        a_max, a_top, a_neg, a_off, a_exp, a_sum, a_den, a_inv = (stats_a[:, 4 * n:4 * n + 4] for n in range(8))
        shared_end = place[0]

        q_b = sb("q_b", [P, 2, SEQ], F32R)
        k_b = sb("k_b", [P, 2, SEQ], F32R)
        k_lo = sb("k_lo", [P, SEQ], F32R)
        v_hi = sb("v_hi", [P, ST, P], F32R)
        v_lo = sb("v_lo", [P, ST, P], F32R)
        x_hi = sb("x_hi", [P, KT, SEQ], F32R)
        x_lo = sb("x_lo", [P, KT, SEQ], F32R)
        logits = sb("logits", [P, 2, 2, SEQ])
        p_hi = sb("p_hi", [P, PT_RING, HALF], F32R)
        p_lo = sb("p_lo", [P, PT_RING, HALF], F32R)
        mk_raw = sb("mk_raw", [P, HEADS, MEM])
        mv_raw = sb("mv_raw", [P, HEADS, 2, P])
        mk_hi = sb("mk_hi", [P, MEM], F32R)
        mk_lo = sb("mk_lo", [P, MEM], F32R)
        mv_hi = sb("mv_hi", [P, 2, P], F32R)
        mv_lo = sb("mv_lo", [P, 2, P], F32R)
        m_probs = sb("m_probs", [P, 2, MEM])
        a_q = sb("a_q", [P, SEQ])
        a_k = sb("a_k", [P, CHUNK + SEQ])
        a_v = sb("a_v", [P, 2 * ST, P])
        a_band = sb("a_band", [P, 4, P])
        a_probs = sb("a_probs", [P, 4, P])
        a_pt = sb("a_pt", [P, 4, P])
        b_out = sb("b_out", [P, CHUNK + SEQ])
        b_bias = sb("b_bias", [P, SEQ + P])
        a_bias = sb("a_bias", [P, 2, 2, P])
        main_end = place[0]
        q_m_hi, q_m_lo = q_b[:, 0, :], q_b[:, 1, :]
        bv_t = b_out[:, 0:SEQ]
        squares = logits[:, 0, 0, :]
        inv_rms = logits[:, 0, 1, :]
        mem_hi = q_b[:, :, :].rearrange("p a n -> p (a n)").rearrange("p (k n) -> p k n", k=KT)
        mem_lo = k_b[:, :, :].rearrange("p a n -> p (a n)").rearrange("p (k n) -> p k n", k=KT)
        rows_raw = [logits[:, 0, 0, :], logits[:, 0, 1, :]]
        rows = [logits[:, 1, 0, :], logits[:, 1, 1, :]]
        g_norm_b, g_mem_b, mv_t = gates["a"], gates["b"], gates["m"]
        av_t = b_out
        lam_in = a_pt[:, :, 0:DK]
        lam_prod = a_band[:, 0:2, 0:DK]

        place[0] = shared_end
        wo = sb("wo", [P, MIX_TILES - 1, 2, D], F32R)
        mix_raw = sb("mix_raw", [P, 2, MIX_TILES, P])
        mix_hi = sb("mix_hi", [P, 2, MIX_TILES, P], F32R)
        mix_lo = sb("mix_lo", [P, 2, MIX_TILES, P], F32R)
        x_res = sb("x_res", [P, 2, D])
        y_row = sb("y_row", [P, 2, D])
        y_sq = sb("y_sq", [P, D])
        g_fin = sb("g_fin", [P, D])
        assert max(place[0], main_end) <= nc.sbuf_usable_end, (place[0], main_end)

        acc = ctx.enter_context(nc.psum_tensor("acc", [P, 2, HALF], F32))
        score = ctx.enter_context(nc.psum_tensor("score", [P, S_RING, HALF], F32))
        trans = ctx.enter_context(nc.psum_tensor("trans", [P, T_RING, HALF], F32))
        mixo = ctx.enter_context(nc.psum_tensor("mixo", [P, HALF], F32))
        y_acc = [acc[:, 0, :], acc[:, 1, :], score[:, 0, :], score[:, 1, :]]

        raw_full = [sem("raw_full0"), sem("raw_full1")]
        w_hi_done = sem("w_hi_done")
        w_lo_done = sem("w_lo_done")
        rows_full = [sem("rows_full0"), sem("rows_full1")]
        consts_full = sem("consts_full")
        gmem_full = sem("gmem_full")
        gnorm_full = sem("gnorm_full")
        rows_std = sem("rows_std")
        rows_sq = sem("rows_sq")
        rows_inv = sem("rows_inv")
        rows_done = sem("rows_done")
        acc_full = sem("acc_full")
        acc_part = sem("acc_part")
        acc_free = sem("acc_free")
        t_full = sem("t_full")
        t_hi = sem("t_hi")
        t_free = sem("t_free")
        s_full = sem("s_full")
        s_free_dve = sem("s_free_dve")
        s_free_act = sem("s_free_act")
        pt_done = sem("pt_done")
        squares_split = sem("squares_split")
        squares_made = sem("squares_made")
        squares_hi = sem("squares_hi")
        a_mixed = sem("a_mixed")
        o_free = sem("o_free")
        bias_made = sem("bias_made")
        b_neg_made = sem("b_neg_made")
        b_exp = sem("b_exp")
        b_inv_made = sem("b_inv_made")
        b_scaled = sem("b_scaled")
        b_ready = sem("b_ready")
        m_max_made = sem("m_max_made")
        m_neg_made = sem("m_neg_made")
        m_inv_made = sem("m_inv_made")
        m_ready = sem("m_ready")
        mkv_hi = sem("mkv_hi")
        mkv_lo = sem("mkv_lo")
        a_max_made = sem("a_max_made")
        a_top_made = sem("a_top_made")
        a_neg_made = sem("a_neg_made")
        a_off_made = sem("a_off_made")
        a_exp_made = sem("a_exp_made")
        a_den_made = sem("a_den_made")
        a_inv_made = sem("a_inv_made")
        a_ready = sem("a_ready")
        gate_tanh = sem("gate_tanh")
        rms_made = sem("rms_made")
        inv_made = sem("inv_made")
        b_normed = sem("b_normed")
        b_gated = sem("b_gated")
        spilled = {g: sem(f"spilled_{g}") for g in "abm"}
        mask_made = sem("mask_made")
        const_made = sem("const_made")
        table_step = sem("table_step")
        lam_exp = sem("lam_exp")
        mix_full = [sem("mix_full0"), sem("mix_full1")]
        mix_last = [sem("mix_last0"), sem("mix_last1")]
        mix_hi_done = sem("mix_hi_done")
        mix_lo_done = sem("mix_lo_done")
        y_full = sem("y_full")
        res_full = [sem("res_full0"), sem("res_full1")]
        gfin_full = sem("gfin_full")
        y_added = [sem("y_added0"), sem("y_added1")]
        y_sqd = sem("y_sqd")
        y_std = sem("y_std")
        y_inv = sem("y_inv")
        y_done = sem("y_done")
        stored = [sem("stored0"), sem("stored1")]

        block = ctx.enter_context(nc.Block())

        def at(number, h, per_turn, before=0):
            return h * per_turn + (before + number + 1)

        def raw_at(n_const, h):
            return h * (NT // 2 * 32) + 32 * ((PRE_TILES + n_const) // 2 + 1)

        def head_loop_over(eng):
            eng.wait_ge(acc_full, PRE_ACC + 2 * NT * HEADS)
            eng.wait_ge(acc_free, PRE_ACC + 2 * NT * HEADS)
            eng.wait_ge(s_full, NS * HEADS)
            eng.wait_ge(s_free_act, len(S_BY_ACT) * HEADS)
            eng.wait_ge(s_free_dve, len(S_BY_DVE) * HEADS)
            eng.wait_ge(t_free, PRE_T + NTB * HEADS)
            eng.wait_ge(pt_done, NMIX * HEADS)
            eng.wait_ge(a_mixed, 4 * HEADS)
            eng.wait_ge(o_free, NO * HEADS)
            eng.wait_ge(b_normed, 2 * HEADS)
            eng.wait_ge(b_gated, 2 * HEADS)

        @block.sync
        def _(sp):
            def load_tile(view, slot, cols, split):
                dst = w_raw[:, slot, :].rearrange("p (k n) -> p k n", k=KT)
                if split is not None:
                    for c in range(2):
                        sp.dma_start(dst[:, :, c * DK:(c + 1) * DK], view[:, :, bass.ds(cols + c * split, DK)])\
                          .then_inc(raw_full[slot], 16)
                else:
                    for c in range(2):
                        ks = slice(c * KT // 2, (c + 1) * KT // 2)
                        sp.dma_start(dst[:, ks, :], view[:, ks, bass.ds(cols, P)]).then_inc(raw_full[slot], 16)

            sp.dma_start(rows_raw[0], mem_rows[:, 0, :]).then_inc(rows_full[0], 16)
            sp.dma_start(rows_raw[1], mem_rows[:, 1, :]).then_inc(rows_full[1], 16)
            sp.dma_start(g_mem_b[:, :], g_mem.partition_broadcast(P)[:, 0, :]).then_inc(gmem_full, 16)
            load_tile(w_mem_v, 0, 0, None)
            load_tile(w_mem_v, 1, 4 * P, None)
            sp.dma_start(g_norm_b[:, :], g_norm.partition_broadcast(P)[:, 0, :]).then_inc(gnorm_full, 16)
            for j, v in enumerate((lq1, lk1, lq2, lk2)):
                sp.dma_start(lam_in[:, j, :], v.partition_broadcast(P)[:, 0, :]).then_inc(consts_full, 16)
            sp.dma_start(sink_in, a_sinks.partition_broadcast(P)[:, 0, :]).then_inc(consts_full, 16)
            sp.dma_start(subln, subln_g.rearrange("l p -> p l")).then_inc(consts_full, 16)
            for par in range(2):
                sp.wait_ge(rows_done, par + 1)
                sp.dma_start(rows_raw[par], x_rows[:, par, :]).then_inc(rows_full[par], 16)
            with sp.Fori(0, 3) as q:
                for par in range(2):
                    sp.wait_ge(w_lo_done, q * 2 + par + 1)
                    load_tile(w_mem_v, par, q * P + (P + 4 * P * par), None)
                    sp.wait_ge(rows_done, q * 2 + par + 3)
                    sp.dma_start(rows_raw[par], x_rows[:, bass.ds(q * 2 + (par + 2), 1), :].rearrange("p a n -> p (a n)"))\
                      .then_inc(rows_full[par], 16)
            for par, col in enumerate((AV, AK)):
                sp.wait_ge(w_lo_done, 7 + par)
                load_tile(w_in_v, par, col, None)
            for w in range(2):
                sp.wait_ge(w_lo_done, PRE_TILES - 1 + w)
                load_tile(w_in_v, w, TILES[w][1], 4 * DK)

            def load_head_tile(w, h):
                name, col, two = TILES[w % NT]
                step = DK if two else P
                sp.wait_ge(w_lo_done, at(w - 2, h, NT, PRE_TILES))
                load_tile(w_in_v, w % 2, h * step + (col + (step if w >= NT else 0)), 4 * DK if two else None)

            def spill(g, h):
                if g == "b":
                    sp.wait_ge(b_gated, h * 2 + 2)
                else:
                    sp.wait_ge(o_free, at(O_AT[(f"{g}_mix", 3)], h, NO))
                sp.dma_start(mixed_v[:, bass.ds(h * 3 + "abm".index(g), 1), :],
                             gates[g][:, :].rearrange("p (a n) -> p a n", a=1)).then_inc(spilled[g], 16)

            with sp.Fori(0, HEADS - 1) as h:
                for w in range(2, NT + 2):
                    load_head_tile(w, h)
                for g in "amb":
                    spill(g, h)
            for w in range(2, NT):
                load_head_tile(w, HEADS - 1)

            n_tiles = PRE_TILES + NT * HEADS

            def load_wo(j):
                t, g = divmod(j, 3)
                first = (t * DK, (512 + t * P), (1024 + t * P))[g]
                second = first + (4 * DK if g == 0 else DK)
                sp.wait_ge(w_lo_done, n_tiles + j - 1)
                for c, row in enumerate((first, second)):
                    sp.dma_start(w_raw[c * DK:(c + 1) * DK, j % 2, :], w_out_v[row:row + DK, :])\
                      .then_inc(raw_full[j % 2], 16)

            def load_mix(par, t):
                cols = bass.ds(t * P, P)
                sp.dma_start(mix_raw[:, par, 0:9, :], mixed_v[:, 0:9, cols]).then_inc(mix_full[par], 16)
                sp.dma_start(mix_raw[:, par, 9:12, :], mixed_v[:, 9:12, cols]).then_inc(mix_last[par], 16)
                sp.dma_start(x_res[:, par:par + 1, :], x_rows[:, bass.ds(t, 1), :]).then_inc(res_full[par], 16)

            load_wo(0)
            load_wo(1)
            for g in "amb":
                spill(g, HEADS - 1)
            head_loop_over(sp)
            for g in "abm":
                sp.wait_ge(spilled[g], 16 * HEADS)
            sp.dma_start(g_fin[:, :], g_final.partition_broadcast(P)).then_inc(gfin_full, 16)
            load_mix(0, 0)
            load_wo(2)
            load_wo(3)
            load_mix(1, 1)
            for j in range(4, MIX_TILES):
                load_wo(j)

            def store(par, z):
                sp.wait_ge(y_done, z * 2 + (par + 1))
                sp.dma_start(y_rows[:, bass.ds(z * 2 + par, 1), :], y_row[:, par:par + 1, :])\
                  .then_inc(stored[par], 16)

            with sp.Fori(0, ST // 2 - 1) as z:
                for par in range(2):
                    sp.wait_ge(mix_lo_done, z * 4 + (2 * par + 2))
                    sp.wait_ge(y_added[par], z * 2 + 2)
                    load_mix(par, z * 2 + (par + 2))
                    store(par, z)
            for par in range(2):
                store(par, ST // 2 - 1)
            for par in range(2):
                sp.wait_ge(stored[par], 16 * ST // 2)

        @block.scalar
        def _(act):
            def split_hi(n):
                slot = n % 2
                act.wait_ge(raw_full[slot], 32 * (n // 2 + 1))
                if n >= 2:
                    act.wait_ge(acc_full, n - 1 if n < PRE_TILES else n)
                act.activation(w_hi[:, slot, :], w_raw[:, slot, :], ACT.Copy).then_inc(w_hi_done, 1)

            def row_stats(par, full, done_before, r):
                act.wait_ge(rows_full[par], full)
                if done_before is not None:
                    act.wait_ge(t_full, done_before)
                act.activation(rows[par], rows_raw[par], ACT.Square, accum_out=ssq[:, par:par + 1])\
                   .then_inc(rows_sq, 1)
                act.wait_ge(rows_sq, r + 1)
                act.activation(std[:, par:par + 1], ssq[:, par:par + 1], ACT.Sqrt, bias=eps, scale=1.0 / D)\
                   .then_inc(rows_std, 1)

            act.wait_ge(const_made, 1)
            for par in range(2):
                row_stats(par, 16, None, par)
            split_hi(0)
            for par in range(2):
                for u in range(2):
                    act.wait_ge(t_full, 2 * par + u + 1)
                    act.activation(mem_hi[:, 4 * u:4 * u + 4, par * P:(par + 1) * P],
                                   trans[:, u, :].rearrange("p (k n) -> p k n", k=4), ACT.Copy).then_inc(t_hi, 1)
            with act.Fori(0, 4) as q:
                for par in range(2):
                    n = 1 - par
                    act.wait_ge(raw_full[n], (q * 32 + 32) if par == 0 else (q * 32 + 64))
                    act.wait_ge(acc_full, q * 2 + par)
                    act.activation(w_hi[:, n, :], w_raw[:, n, :], ACT.Copy).then_inc(w_hi_done, 1)
                    row_stats(par, q * 16 + 32, q * 4 + (2 + 2 * par), q * 2 + (par + 2))
                    for u in range(2):
                        act.wait_ge(t_full, q * 4 + (5 + 2 * par + u))
                        act.activation(x_hi[:, 4 * u:4 * u + 4, bass.ds(q * 2 * P + par * P, P)],
                                       trans[:, u, :].rearrange("p (k n) -> p k n", k=4), ACT.Copy)\
                           .then_inc(t_hi, 1)
            act.wait_ge(table_step, 2)
            act.activation(lam_exps, lam_sums, ACT.Exp).then_inc(lam_exp, 1)
            split_hi(9)
            split_hi(10)

            with act.Fori(0, HEADS) as h:
                def start():
                    act.wait_ge(t_free, 22)
                    act.wait_ge(s_full, h * NS)
                    act.wait_ge(pt_done, h * NMIX)
                    act.activation(mk_hi[:, :], mk_raw[:, bass.ds(h, 1), :].rearrange("p a n -> p (a n)"), ACT.Copy)\
                       .then_inc(mkv_hi, 1)
                    act.activation(mv_hi[:, :, :].rearrange("p a n -> p (a n)"),
                                   mv_raw[:, bass.ds(h, 1), :, :].rearrange("p h a n -> p (h a n)"), ACT.Copy)\
                       .then_inc(mkv_hi, 1)

                def weights(w):
                    slot = w % 2
                    act.wait_ge(raw_full[slot], raw_at(w, h))
                    act.wait_ge(acc_full, at(2 * w - 3, h, 2 * NT, PRE_ACC))
                    act.activation(w_hi[:, slot, :], w_raw[:, slot, :], ACT.Copy).then_inc(w_hi_done, 1)

                def evacuate(w, s):
                    name = TILES[w][0]
                    cols = slice(s * HALF, (s + 1) * HALF)
                    if name in ("bv", "aq"):
                        return
                    act.wait_ge(acc_full, at(2 * w + s, h, 2 * NT, PRE_ACC))
                    if name == "bk":
                        for c in range(2):
                            for half in range(2):
                                act.activation(k_b[half * DK:(half + 1) * DK, c, cols],
                                               acc[c * DK:(c + 1) * DK, s, :], ACT.Copy).then_inc(acc_part, 1)
                    elif name == "bq":
                        for c in range(2):
                            act.activation(q_b[c * DK:(c + 1) * DK, c, cols], acc[c * DK:(c + 1) * DK, s, :],
                                           ACT.Copy, scale=QK_SCALE).then_inc(acc_part, 1)
                    elif name == "mq":
                        act.wait_ge(s_full, at(S_AT[("b", 7, 1, 1)], h, NS))
                        act.activation(q_m_hi[:, cols], acc[:, s, :], ACT.Copy).then_inc(acc_part, 1)
                    else:
                        g = name[0]
                        act.wait_ge(spilled[g], h * 16)
                        act.activation(gates[g][:, cols], acc[:, s, :], ACT.Tanh, scale=0.5).then_inc(acc_part, 1)

                def b_scores(i):
                    width = sum(n for _, n in b_pieces(i))
                    act.wait_ge(b_neg_made, at(i, h, ST))
                    for c in range(2):
                        act.activation(logits[:, i % 2, c, 0:width], logits[:, i % 2, c, 0:width], ACT.Exp,
                                       bias=b_neg[:, 2 * (i % 2) + c:2 * (i % 2) + c + 1],
                                       accum_out=b_sum[:, 2 * (i % 2) + c:2 * (i % 2) + c + 1])\
                           .then_inc(b_exp, 1)

                def take_hi(step, out):
                    bank = T_AT[step] % T_RING
                    act.wait_ge(t_full, at(T_AT[step], h, NTB, PRE_T))
                    act.activation(out, trans[:, bank, :], ACT.Copy).then_inc(t_hi, 1)

                def v_spread(half):
                    if half == 0:
                        act.wait_ge(pt_done, h * NMIX)
                    take_hi(("v_spread", half), v_hi[:, 4 * half:4 * half + 4, :].rearrange("p j n -> p (j n)"))

                def p_slot_free(n):
                    if n < PT_RING:
                        act.wait_ge(pt_done, h * NMIX)
                        act.wait_ge(t_full, h * NTB + PRE_T)
                        return
                    last = list(PT_AT)[n - PT_RING]
                    if last in PT_MIX:
                        act.wait_ge(pt_done, at(PT_MIX[last], h, NMIX))
                    else:
                        act.wait_ge(t_full, at(T_AT[last], h, NTB, PRE_T))

                def p_spread(step):
                    n = PT_AT[step]
                    p_slot_free(n)
                    take_hi(step, p_hi[:, n % PT_RING, :])

                def m_norm(m):
                    act.wait_ge(m_neg_made, at(m, h, 4))
                    bank = S_AT[("m", m)] % S_RING
                    if m > 0:
                        act.wait_ge(t_full, at(T_AT[("m_spread", m - 1)], h, NTB, PRE_T))
                    else:
                        act.wait_ge(t_full, h * NTB + PRE_T)
                    act.activation(m_probs[:, 0, :], score[:, bank, 0:MEM], ACT.Exp, bias=m_neg[:, 0:1],
                                   scale=M_SCALE, accum_out=m_sum[:, 0:1])
                    act.activation(m_probs[:, 1, :], score[:, bank, MEM:2 * MEM], ACT.Exp, bias=m_neg[:, 1:2],
                                   scale=M_SCALE, accum_out=m_sum[:, 1:2]).then_inc(s_free_act, 1)

                def a_scores(m):
                    act.wait_ge(a_off_made, at(m, h, 4))
                    for n in range(4):
                        act.activation(a_band[:, n, :], a_band[:, n, :], ACT.Exp, bias=a_neg[:, n:n + 1],
                                       accum_out=a_sum[:, n:n + 1])
                    act.activation(a_exp, a_off, ACT.Exp).then_inc(a_exp_made, 1)

                def b_squares(s):
                    n = PT_AT[("b_squares", s)]
                    act.wait_ge(squares_made, at(s, h, 2))
                    p_slot_free(n)
                    act.activation(p_hi[:, n % PT_RING, :], squares[:, s * HALF:(s + 1) * HALF], ACT.Copy)\
                       .then_inc(squares_hi, 1)

                def b_finish(s):
                    cols = slice(s * HALF, (s + 1) * HALF)
                    act.wait_ge(t_free, at(T_AT[("b_squares", s)], h, NTB, PRE_T))
                    act.activation(inv_rms[:, cols], inv_rms[:, cols], ACT.Sqrt).then_inc(rms_made, 1)

                for s in HEAD:
                    if s[0] == "start":
                        start()
                    elif s[0] == "weights":
                        weights(s[1])
                    elif s[0] == "evacuate":
                        evacuate(*s[1:])
                    elif s[0] == "b_scores":
                        b_scores(s[1])
                    elif s[0] in ("b_spread", "m_spread"):
                        p_spread(s)
                    elif s[0] == "v_spread":
                        v_spread(s[1])
                    elif s[0] == "m_norm":
                        m_norm(s[1])
                    elif s[0] == "a_scores":
                        a_scores(s[1])
                    elif s[0] == "b_squares":
                        b_squares(s[1])
                    elif s[0] == "b_finish":
                        b_finish(s[1])

            def mix_split(par, full, used):
                if used is not None:
                    act.wait_ge(y_full, used)
                act.wait_ge(mix_full[par], full)
                act.activation(mix_hi[:, par, 0:9, :], mix_raw[:, par, 0:9, :], ACT.Copy).then_inc(mix_hi_done, 1)
                act.wait_ge(mix_last[par], full)
                act.activation(mix_hi[:, par, 9:12, :], mix_raw[:, par, 9:12, :], ACT.Copy)\
                   .then_inc(mix_hi_done, 1)

            head_loop_over(act)
            n_tiles = PRE_TILES + NT * HEADS
            for j in range(1, MIX_TILES):
                act.wait_ge(raw_full[j % 2], 32 * ((n_tiles + j) // 2 + 1))
                act.activation(wo[:, j - 1, 0, :], w_raw[:, j % 2, :], ACT.Copy).then_inc(w_hi_done, 1)
                if j == 1:
                    mix_split(0, 16, None)
                if j == 6:
                    mix_split(1, 16, None)

            def finish_row(par, z):
                act.wait_ge(y_added[par], z * 2 + 2)
                act.activation(y_sq[:, :], y_row[:, par, :], ACT.Square, accum_out=ssq[:, par:par + 1])\
                   .then_inc(y_sqd, 1)
                act.wait_ge(y_sqd, z * 2 + (par + 1))
                act.activation(std[:, par:par + 1], ssq[:, par:par + 1], ACT.Sqrt, bias=eps, scale=1.0 / D)\
                   .then_inc(y_std, 1)

            with act.Fori(0, ST // 2 - 1) as z:
                for par in range(2):
                    finish_row(par, z)
                    mix_split(par, z * 16 + 32, z * 2 + (par + 1))
            for par in range(2):
                finish_row(par, ST // 2 - 1)

        @block.gpsimd
        def _(pool):
            pool.memset(eps, EPS).then_inc(const_made, 1)
            pool.memset(ident[:, :], 0.0).then_inc(mask_made, 1)
            pool.wait_ge(mask_made, 1)
            pool.affine_select(out=ident[:, :], in_=ident[:, :], compare_op=ALU.not_equal, fill=1.0,
                               base=0, pattern=[[-1, P]], channel_multiplier=1).then_inc(const_made, 1)
            pool.memset(a_k[:, 0:CHUNK], 0.0).then_inc(const_made, 1)
            pool.iota(b_bias[:, :], [[1, SEQ + P]], base=-(SEQ - P), channel_multiplier=-1,
                      allow_small_or_imprecise_dtypes=True).then_inc(const_made, 1)
            pool.iota(a_bias[:, :, :, :], [[0, 4], [1, P]], base=-CHUNK, channel_multiplier=-1,
                      allow_small_or_imprecise_dtypes=True).then_inc(const_made, 1)

            def split_lo(slot, n):
                pool.wait_ge(w_hi_done, n + 1)
                pool.tensor_tensor(w_lo[:, slot, :], w_raw[:, slot, :], w_hi[:, slot, :].bitcast(F32),
                                   ALU.subtract).then_inc(w_lo_done, 1)

            pool.memset(av_t[:, 0:CHUNK], 0.0).then_inc(const_made, 1)
            split_lo(0, 0)
            with pool.Fori(0, 4) as q:
                for par in range(2):
                    split_lo(1 - par, q * 2 + (1 + par))
            split_lo(1, 9)
            split_lo(0, 10)

            with pool.Fori(0, HEADS) as h:
                def start():
                    pool.wait_ge(mkv_hi, h * 2 + 2)
                    pool.tensor_tensor(mk_lo[:, :], mk_raw[:, bass.ds(h, 1), :].rearrange("p a n -> p (a n)"),
                                       mk_hi[:, :].bitcast(F32), ALU.subtract).then_inc(mkv_lo, 1)
                    pool.tensor_tensor(mv_lo[:, :, :].rearrange("p a n -> p (a n)"),
                                       mv_raw[:, bass.ds(h, 1), :, :].rearrange("p h a n -> p (h a n)"),
                                       mv_hi[:, :, :].rearrange("p a n -> p (a n)").bitcast(F32), ALU.subtract)\
                        .then_inc(mkv_lo, 1)

                def b_combine(i):
                    width = sum(n for _, n in b_pieces(i))
                    pool.wait_ge(b_inv_made, at(i, h, ST))
                    pool.nop(nofuse=True)
                    pool.tensor_scalar(logits[:, i % 2, 1, 0:width], logits[:, i % 2, 1, 0:width],
                                       b_inv[:, 2 * (i % 2) + 1:2 * (i % 2) + 2], neg_lam, ALU.mult, ALU.mult)\
                        .then_inc(b_scaled, 1)

                def m_norm(m):
                    pool.wait_ge(m_inv_made, at(m, h, 4))
                    pool.tensor_tensor(m_probs[:, :, :], m_probs[:, :, :],
                                       m_inv.rearrange("p (a n) -> p a n", n=1).broadcast_to([P, 2, MEM]), ALU.mult)\
                        .then_inc(m_ready, 1)

                def a_norm(m):
                    pool.wait_ge(a_inv_made, at(m, h, 4))
                    if m > 0:
                        pool.wait_ge(t_full, at(T_AT[("a_spread", m - 1)], h, NTB, PRE_T))
                    else:
                        pool.wait_ge(t_full, h * NTB + PRE_T)
                    pool.tensor_tensor(a_probs[:, :, :], a_band[:, :, :],
                                       a_inv.rearrange("p (a n) -> p a n", n=1).broadcast_to([P, 4, P]), ALU.mult)\
                        .then_inc(a_ready, 1)

                def b_squares(s):
                    cols = slice(s * HALF, (s + 1) * HALF)
                    n = PT_AT[("b_squares", s)]
                    pool.wait_ge(o_free, at(O_AT[("b_mix", 2 * s + 1)], h, NO))
                    pool.wait_ge(t_full, at(T_AT[("b_spread", 3, 3)], h, NTB, PRE_T))
                    pool.tensor_tensor(squares[:, cols], b_out[:, cols], b_out[:, cols], ALU.mult)\
                        .then_inc(squares_made, 1)
                    pool.wait_ge(squares_hi, at(s, h, 2))
                    pool.tensor_tensor(p_lo[:, n % PT_RING, :], squares[:, cols],
                                       p_hi[:, n % PT_RING, :].bitcast(F32), ALU.subtract)\
                        .then_inc(squares_split, 1)

                def b_finish(s):
                    cols = slice(s * HALF, (s + 1) * HALF)
                    pool.wait_ge(inv_made, at(s, h, 2))
                    pool.tensor_tensor(b_out[:, cols], b_out[:, cols], inv_rms[:, cols], ALU.mult)\
                        .then_inc(b_normed, 1)

                for s in HEAD:
                    if s[0] == "start":
                        start()
                    elif s[0] == "weights":
                        split_lo(s[1] % 2, h * NT + (PRE_TILES + s[1]))
                    elif s[0] == "b_combine":
                        b_combine(s[1])
                    elif s[0] == "m_norm":
                        m_norm(s[1])
                    elif s[0] == "a_norm":
                        a_norm(s[1])
                    elif s[0] == "b_squares":
                        b_squares(s[1])
                    elif s[0] == "b_finish":
                        b_finish(s[1])

            def mix_split(par, n):
                for part, js in enumerate((slice(0, 9), slice(9, 12))):
                    pool.wait_ge(mix_hi_done, n * 2 + (part + 1))
                    pool.tensor_tensor(mix_lo[:, par, js, :], mix_raw[:, par, js, :],
                                       mix_hi[:, par, js, :].bitcast(F32), ALU.subtract).then_inc(mix_lo_done, 1)

            for j in range(1, MIX_TILES):
                pool.wait_ge(w_hi_done, PRE_TILES + NT * HEADS + j + 1)
                pool.tensor_tensor(wo[:, j - 1, 1, :], w_raw[:, j % 2, :], wo[:, j - 1, 0, :].bitcast(F32),
                                   ALU.subtract).then_inc(w_lo_done, 1)
                if j == 1:
                    mix_split(0, 0)
                if j == 6:
                    mix_split(1, 1)
            with pool.Fori(0, ST // 2 - 1) as z:
                for par in range(2):
                    mix_split(par, z * 2 + (2 + par))

        @block.vector
        def _(dve):
            steps = [0]

            def table(ins):
                steps[0] += 1
                ins.then_inc(table_step, 1)
                dve.wait_ge(table_step, steps[0])

            dve.wait_ge(gmem_full, 16)

            def normalise(par, gain, r):
                dve.wait_ge(rows_std, r + 1)
                dve.reciprocal(rstd[:, par:par + 1], std[:, par:par + 1]).then_inc(rows_inv, 1)
                dve.wait_ge(rows_inv, r + 1)
                dve.scalar_tensor_tensor(out=rows[par], in0=rows_raw[par], scalar=rstd[:, par:par + 1],
                                         in1=gain[:, :], op0=ALU.mult, op1=ALU.mult).then_inc(rows_done, 1)

            for par in range(2):
                normalise(par, g_mem_b, par)
            for par in range(2):
                for u in range(2):
                    dve.wait_ge(t_hi, 2 * par + u + 1)
                    out = slice(4 * u, 4 * u + 4), slice(par * P, (par + 1) * P)
                    dve.tensor_tensor(mem_lo[:, out[0], out[1]], trans[:, u, :].rearrange("p (k n) -> p k n", k=4),
                                      mem_hi[:, out[0], out[1]].bitcast(F32), ALU.subtract).then_inc(t_free, 1)
            dve.wait_ge(gnorm_full, 16)
            with dve.Fori(0, 4) as q:
                for par in range(2):
                    normalise(par, g_norm_b, q * 2 + (2 + par))
                    dve.wait_ge(acc_full, q * 2 + (par + 1))
                    out = mk_raw[:, bass.ds(q, 1), :].rearrange("p a n -> p (a n)") if par == 0 else \
                        mv_t[:, bass.ds(q * MEM, MEM)]
                    dve.tensor_copy(out, acc[:, par, 0:MEM]).then_inc(acc_free, 1)
                    for u in range(2):
                        dve.wait_ge(t_hi, q * 4 + (5 + 2 * par + u))
                        cols = bass.ds(q * 2 * P + par * P, P)
                        dve.tensor_tensor(x_lo[:, 4 * u:4 * u + 4, cols],
                                          trans[:, u, :].rearrange("p (k n) -> p k n", k=4),
                                          x_hi[:, 4 * u:4 * u + 4, cols].bitcast(F32), ALU.subtract)\
                           .then_inc(t_free, 1)
            dve.wait_ge(consts_full, 96)
            table(dve.tensor_tensor(lam_prod, lam_in[:, 0:4:2, :], lam_in[:, 1:4:2, :], ALU.mult))
            table(dve.reduce_sum(lam_sums, lam_prod, AX.X))
            for i in range(2):
                table(dve.tensor_copy(sinks.rearrange("p (t g i) -> p t g i", t=4, g=2)[:, :, :, i],
                                      sink_in.rearrange("p (g t) -> p t g", g=2)))
            for s in range(2):
                dve.wait_ge(acc_full, 9 + s)
                dve.tensor_copy(av_t[:, CHUNK + s * HALF:CHUNK + (s + 1) * HALF], acc[:, s, :]).then_inc(acc_free, 1)
            for v in range(2):
                dve.wait_ge(t_full, 21 + v)
                dve.tensor_copy(mv_raw[:, 2 * v:2 * v + 2, :, :].rearrange("p h a n -> p (h a n)"), trans[:, v, :])\
                   .then_inc(t_free, 1)
            dve.wait_ge(lam_exp, 1)
            table(dve.tensor_tensor(neg_lam, lam_exps[:, 1:2], lam_exps[:, 0:1], ALU.subtract))
            table(dve.tensor_scalar(neg_lam, neg_lam, -LAM_INIT, None, ALU.add))
            table(dve.tensor_scalar(subln, subln, 0.5 * (1.0 - LAM_INIT), None, ALU.mult))
            dve.memset(ones[:, :].bitcast(F32), 1.0).then_inc(table_step, 1)
            steps[0] += 1
            dve.wait_ge(const_made, 5)
            table(dve.tensor_scalar(a_bias[CHUNK:P, :, :, :], a_bias[CHUNK:P, :, :, :], float(CHUNK), None, ALU.add))
            for t in (b_bias[:, :], a_bias[:, :, :, :].rearrange("p g t n -> p (g t n)")):
                table(dve.scalar_tensor_tensor(out=t, in0=t, scalar=-1.0, in1=t, op0=ALU.mult, op1=ALU.min))
            table(dve.tensor_scalar(a_bias[:, 1, :, :], a_bias[:, 1, :, :], 2.0 ** -4, None, ALU.mult))
            masks = [b_bias[0:CHUNK, SEQ - P + CHUNK:SEQ + P], b_bias[CHUNK:P, SEQ:SEQ + P],
                     a_bias[0:CHUNK, :, 0, 0:CHUNK]]
            for m in masks:
                table(dve.memset(m, MASKED))
            for s in range(2):
                dve.wait_ge(acc_full, 11 + s)
                dve.tensor_copy(a_k[:, CHUNK + s * HALF:CHUNK + (s + 1) * HALF], acc[:, s, :]).then_inc(acc_free, 1)
            for v in range(4):
                dve.wait_ge(t_full, 23 + v)
                dve.tensor_copy(a_v[:, 4 * v:4 * v + 4, :].rearrange("p c n -> p (c n)"), trans[:, v % 2, :])\
                   .then_inc(t_free, 1)

            with dve.Fori(0, HEADS) as h:
                def start():
                    dve.wait_ge(s_free_dve, h * len(S_BY_DVE))
                    dve.tensor_scalar(b_bias[:, :], b_bias[:, :], 0.25, None, ALU.mult).then_inc(bias_made, 1)
                    dve.tensor_scalar(a_bias[:, :, :, :], a_bias[:, :, :, :], 0.5, None, ALU.mult)\
                       .then_inc(bias_made, 1)
                    dve.wait_ge(bias_made, h * 2 + 2)

                parts = {"bk": 4, "bq": 2, "bv": 0, "aq": 0, "ag": 1, "mq": 1, "mg": 1, "bg": 1}
                per_turn = 2 * sum(parts.values())
                before = {}
                n = 0
                for w, (name, _, _) in enumerate(TILES):
                    for s in range(2):
                        n += parts[name]
                        before[(w, s)] = n

                def evacuate(w, s):
                    name = TILES[w][0]
                    cols = slice(s * HALF, (s + 1) * HALF)
                    if name == "bv":
                        dve.wait_ge(b_gated, h * 2)
                    if parts[name]:
                        dve.wait_ge(acc_part, h * per_turn + before[(w, s)])
                    else:
                        dve.wait_ge(acc_full, at(2 * w + s, h, 2 * NT, PRE_ACC))
                    if name == "bk":
                        for c in range(2):
                            ps = slice(c * DK, (c + 1) * DK)
                            last = dve.tensor_tensor(k_lo[ps, cols], acc[ps, s, :], k_b[ps, c, cols].bitcast(F32),
                                                     ALU.subtract)
                    elif name == "bq":
                        for c in range(2):
                            ps = slice(c * DK, (c + 1) * DK)
                            po = slice((1 - c) * DK, (2 - c) * DK)
                            last = dve.scalar_tensor_tensor(out=q_b[po, c, cols], in0=acc[ps, s, :], scalar=QK_SCALE,
                                                            in1=q_b[ps, c, cols].bitcast(F32), op0=ALU.mult,
                                                            op1=ALU.subtract)
                    elif name == "bv":
                        last = dve.tensor_copy(bv_t[:, cols], acc[:, s, :])
                    elif name == "aq":
                        last = dve.tensor_scalar(a_q[:, cols], acc[:, s, :], QK_SCALE, None, ALU.mult)
                    elif name == "mq":
                        last = dve.tensor_tensor(q_m_lo[:, cols], acc[:, s, :], q_m_hi[:, cols].bitcast(F32),
                                                 ALU.subtract)
                    else:
                        g = gates[name[0]]
                        last = dve.scalar_tensor_tensor(out=g[:, cols], in0=g[:, cols], scalar=1.0,
                                                        in1=acc[:, s, :], op0=ALU.add, op1=ALU.mult)
                    last.then_inc(acc_free, 1)

                def b_scores(i):
                    if i >= 2:
                        g = i // 2 - 1
                        dve.wait_ge(t_full, at(T_AT[("b_spread", g, g)], h, NTB, PRE_T))
                    else:
                        dve.wait_ge(t_full, h * NTB + PRE_T)
                        dve.wait_ge(b_normed, h * 2)
                    pieces = b_pieces(i)
                    if i >= 1:
                        dve.wait_ge(b_neg_made, at(i - 1, h, ST))
                    for p, (a, n) in enumerate(pieces):
                        for c in range(2):
                            unit = S_AT[("b", i, p, c)]
                            dve.wait_ge(s_full, at(unit, h, NS))
                            dve.nop(nofuse=True)
                            rel = SEQ - P - i * P + a
                            dve.tensor_tensor_reduce(out=logits[:, i % 2, c, a:a + n],
                                                     in0=score[:, unit % S_RING, 0:n], in1=b_bias[:, rel:rel + n],
                                                     scale=1.0, scalar=-3e38, op0=ALU.add, op1=ALU.max,
                                                     accum_out=b_max[:, 2 * c + p:2 * c + p + 1])\
                               .then_inc(s_free_dve, 1)
                    dve.wait_ge(s_free_dve, at(S_BY_DVE[("b", i, len(pieces) - 1, 1)], h, len(S_BY_DVE)))
                    dve.tensor_reduce(b_neg[:, 2 * (i % 2):2 * (i % 2) + 2],
                                      b_max.rearrange("p (c n) -> p c n", c=2)[:, :, 0:len(pieces)],
                                      axis=AX.X, op=ALU.max, negate=True).then_inc(b_neg_made, 1)

                def b_combine(i):
                    width = sum(n for _, n in b_pieces(i))
                    k = 2 * (i % 2)
                    dve.wait_ge(b_exp, at(2 * i + 1, h, 2 * ST))
                    dve.reciprocal(b_inv[:, k:k + 2], b_sum[:, k:k + 2]).then_inc(b_inv_made, 1)
                    dve.wait_ge(b_inv_made, at(i, h, ST))
                    dve.wait_ge(b_scaled, at(i, h, ST))
                    dve.scalar_tensor_tensor(out=logits[:, i % 2, 0, 0:width], in0=logits[:, i % 2, 0, 0:width],
                                             scalar=b_inv[:, k:k + 1], in1=logits[:, i % 2, 1, 0:width],
                                             op0=ALU.mult, op1=ALU.add).then_inc(b_ready, 1)

                def take_lo(step, out, hi):
                    dve.wait_ge(t_hi, at(T_SPLIT[step], h, len(T_SPLIT), 20))
                    dve.tensor_tensor(out, trans[:, T_AT[step] % T_RING, :], hi.bitcast(F32), ALU.subtract)\
                       .then_inc(t_free, 1)

                def gate(g, m):
                    cols = slice(m * MEM, (m + 1) * MEM)
                    if g == "a":
                        dve.wait_ge(a_mixed, at(m, h, 4))
                    else:
                        dve.wait_ge(pt_done, at(PT_MIX[("m_spread", m)], h, NMIX))
                    w = [n for n, _, _ in TILES].index(f"{g}g")
                    dve.wait_ge(acc_free, at(2 * w + m // 2, h, 2 * NT, PRE_ACC))
                    dve.scalar_tensor_tensor(out=gates[g][:, cols], in0=mixo[:, 0:MEM], scalar=0.5,
                                             in1=gates[g][:, cols], op0=ALU.mult, op1=ALU.mult)\
                       .then_inc(o_free, 1)

                def b_take(g):
                    if g == 0:
                        dve.wait_ge(t_full, at(T_AT[("v_spread", 1)], h, NTB, PRE_T))
                    dve.wait_ge(pt_done, at(PT_MIX[("b_spread", g, g)], h, NMIX))
                    dve.tensor_copy(b_out[:, g * MEM:(g + 1) * MEM], mixo[:, 0:MEM]).then_inc(o_free, 1)

                def m_scores(m):
                    unit = S_AT[("m", m)]
                    dve.wait_ge(s_full, at(unit, h, NS))
                    dve.tensor_reduce(m_max, score[:, unit % S_RING, :].rearrange("p (a n) -> p a n", a=2),
                                      axis=AX.X, op=ALU.max).then_inc(m_max_made, 1)
                    dve.wait_ge(m_max_made, at(m, h, 4))
                    dve.wait_ge(m_ready, at(m - 1, h, 4) if m else h * 4)
                    dve.tensor_scalar(m_neg, m_max, -M_SCALE, None, ALU.mult).then_inc(m_neg_made, 1)

                def m_norm(m):
                    dve.wait_ge(s_free_act, at(m, h, 4))
                    dve.reciprocal(m_inv, m_sum).then_inc(m_inv_made, 1)

                def a_scores(m):
                    dve.wait_ge(a_ready, at(m - 1, h, 4) if m else h * 4)
                    for g in range(2):
                        unit = S_AT[("a", m, g)]
                        dve.wait_ge(s_full, at(unit, h, NS))
                        s = score[:, unit % S_RING, :].rearrange("p (i n) -> p i n", i=2)
                        for c in range(2):
                            ps = slice(c * CHUNK, (c + 1) * CHUNK)
                            bias = a_bias[ps, g, 0:2, :] if m == 0 else \
                                a_bias[ps, g, 1:2, :].broadcast_to([CHUNK, 2, P])
                            last = dve.tensor_tensor(a_band[ps, 2 * g:2 * g + 2, :], s[ps, :, c * CHUNK:c * CHUNK + P],
                                                     bias, ALU.add)
                        last.then_inc(s_free_dve, 1)
                    dve.wait_ge(s_free_dve, at(S_BY_DVE[("a", m, 1)], h, len(S_BY_DVE)))
                    dve.reduce_max(a_max, a_band[:, :, :], AX.X).then_inc(a_max_made, 1)
                    dve.wait_ge(a_max_made, at(m, h, 4))
                    sink = sinks[:, bass.ds(h * 4, 4)]
                    dve.tensor_tensor(a_top, a_max, sink, ALU.max).then_inc(a_top_made, 1)
                    dve.wait_ge(a_top_made, at(m, h, 4))
                    dve.tensor_scalar(a_neg, a_top, -1.0, None, ALU.mult).then_inc(a_neg_made, 1)
                    dve.wait_ge(a_neg_made, at(m, h, 4))
                    dve.tensor_tensor(a_off, sink, a_neg, ALU.add).then_inc(a_off_made, 1)

                def a_norm(m):
                    dve.wait_ge(a_exp_made, at(m, h, 4))
                    dve.tensor_tensor(a_den, a_sum, a_exp, ALU.add).then_inc(a_den_made, 1)
                    dve.wait_ge(a_den_made, at(m, h, 4))
                    dve.reciprocal(a_inv, a_den).then_inc(a_inv_made, 1)

                def a_spread(m):
                    step = ("a_spread", m)
                    dve.wait_ge(t_full, at(T_AT[step], h, NTB, PRE_T))
                    dve.wait_ge(a_mixed, at(m - 1, h, 4) if m else h * 4)
                    dve.tensor_copy(a_pt[:, :, :].rearrange("p a n -> p (a n)"), trans[:, T_AT[step] % T_RING, :])\
                       .then_inc(t_free, 1)

                def b_squares(s):
                    cols = slice(s * HALF, (s + 1) * HALF)
                    step = ("b_squares", s)
                    dve.wait_ge(t_full, at(T_AT[step], h, NTB, PRE_T))
                    dve.tensor_scalar(inv_rms[:, cols], trans[:, T_AT[step] % T_RING, :], 1.0 / P, EPS,
                                      ALU.mult, ALU.add).then_inc(t_free, 1)

                def b_finish(s):
                    cols = slice(s * HALF, (s + 1) * HALF)
                    dve.wait_ge(rms_made, at(s, h, 2))
                    dve.reciprocal(inv_rms[:, cols], inv_rms[:, cols]).then_inc(inv_made, 1)

                def b_gate():
                    for s in range(2):
                        cols = slice(s * HALF, (s + 1) * HALF)
                        dve.wait_ge(b_normed, at(s, h, 2))
                        dve.wait_ge(acc_free, at(2 * (NT - 1) + s, h, 2 * NT, PRE_ACC))
                        dve.scalar_tensor_tensor(out=gates["b"][:, cols], in0=b_out[:, cols], scalar=subln,
                                                 in1=gates["b"][:, cols], op0=ALU.mult, op1=ALU.mult)\
                           .then_inc(b_gated, 1)

                for s in HEAD:
                    if s[0] == "start":
                        start()
                    elif s[0] == "evacuate":
                        evacuate(*s[1:])
                    elif s[0] == "b_scores":
                        b_scores(s[1])
                    elif s[0] == "b_combine":
                        b_combine(s[1])
                    elif s[0] == "v_spread":
                        half = s[1]
                        take_lo(s, v_lo[:, 4 * half:4 * half + 4, :].rearrange("p j n -> p (j n)"),
                                v_hi[:, 4 * half:4 * half + 4, :].rearrange("p j n -> p (j n)"))
                    elif s[0] in ("b_spread", "m_spread"):
                        slot = PT_AT[s] % PT_RING
                        take_lo(s, p_lo[:, slot, :], p_hi[:, slot, :])
                    elif s[0] == "b_mix":
                        if s[1] == s[2]:
                            b_take(s[1])
                    elif s[0] in ("m_mix", "a_mix"):
                        gate(s[0][0], s[1])
                    elif s[0] == "m_scores":
                        m_scores(s[1])
                    elif s[0] == "m_norm":
                        m_norm(s[1])
                    elif s[0] == "a_scores":
                        a_scores(s[1])
                    elif s[0] == "a_norm":
                        a_norm(s[1])
                    elif s[0] == "a_spread":
                        a_spread(s[1])
                    elif s[0] == "b_squares":
                        b_squares(s[1])
                    elif s[0] == "b_finish":
                        b_finish(s[1])
                    elif s[0] == "b_gate":
                        b_gate()

            def finish(par, z):
                dve.wait_ge(y_full, z * 2 + (par + 1))
                dve.wait_ge(res_full[par], z * 16 + 16)
                dve.wait_ge(stored[par], z * 16)
                for s in range(2):
                    cols = slice(s * HALF, (s + 1) * HALF)
                    dve.tensor_tensor(y_row[:, par, cols], y_acc[2 * par + s], x_res[:, par, cols], ALU.add)\
                       .then_inc(y_added[par], 1)
                dve.wait_ge(y_std, z * 2 + (par + 1))
                dve.reciprocal(rstd[:, par:par + 1], std[:, par:par + 1]).then_inc(y_inv, 1)
                dve.wait_ge(y_inv, z * 2 + (par + 1))
                dve.scalar_tensor_tensor(out=y_row[:, par, :], in0=y_row[:, par, :], scalar=rstd[:, par:par + 1],
                                         in1=g_fin[:, :], op0=ALU.mult, op1=ALU.mult).then_inc(y_done, 1)

            dve.wait_ge(gfin_full, 16)
            with dve.Fori(0, ST // 2) as z:
                for par in range(2):
                    finish(par, z)

        @block.tensor
        def _(pe):
            def product(out, a_hi, a_lo, b_hi, b_lo, start, stop):
                pe.matmul(out, a_hi, b_hi, start=start, stop=False, skip_group_check=True)
                pe.matmul(out, a_hi, b_lo, start=False, stop=False, skip_group_check=True)
                return pe.matmul(out, a_lo, b_hi, start=False, stop=stop, skip_group_check=True)

            def spread_rows(par, u):
                for k in range(4):
                    last = pe.transpose(trans[:, u, k * P:(k + 1) * P], rows[par][:, (4 * u + k) * P:(4 * u + k + 1) * P],
                                        ident[:, :])
                last.then_inc(t_full, 1)

            pe.wait_ge(const_made, 2)
            for par in range(2):
                pe.wait_ge(rows_done, par + 1)
                for u in range(2):
                    if par:
                        pe.wait_ge(t_free, u + 1)
                    spread_rows(par, u)
            pe.wait_ge(t_free, 4)
            with pe.Fori(0, 4) as q:
                for par in range(2):
                    pe.wait_ge(w_lo_done, q * 2 + (par + 1))
                    pe.wait_ge(acc_free, q * 2)
                    for k in range(KT):
                        w = slice(k * P, (k + 1) * P)
                        last = product(acc[:, par, 0:MEM], w_hi[:, par, w], w_lo[:, par, w], mem_hi[:, k, :],
                                       mem_lo[:, k, :], k == 0, k == KT - 1)
                    last.then_inc(acc_full, 1)
                    pe.wait_ge(rows_done, q * 2 + (par + 3))
                    for u in range(2):
                        pe.wait_ge(t_free, q * 4 + (2 * par + u + 3))
                        spread_rows(par, u)

            def project(w, s, k):
                tile = slice(k * P, (k + 1) * P)
                cols = slice(s * HALF, (s + 1) * HALF)
                return product(acc[:, s, :], w_hi[:, w % 2, tile], w_lo[:, w % 2, tile], x_hi[:, k, cols],
                               x_lo[:, k, cols], k == 0, k == KT - 1)

            for n in (8, 9):
                pe.wait_ge(w_lo_done, n + 1)
                for s in range(2):
                    unit = 8 + 2 * (n - 8) + s
                    pe.wait_ge(acc_free, unit - 1)
                    pe.wait_ge(t_free, 12 + 8 * s)
                    for k in range(KT):
                        last = project(n, s, k)
                    last.then_inc(acc_full, 1)
                if n == 8:
                    for v in range(2):
                        pe.wait_ge(t_free, 19 + v)
                        for b in range(4):
                            last = pe.transpose(trans[:, v, b * P:(b + 1) * P],
                                                mv_t[:, (4 * v + b) * P:(4 * v + b + 1) * P], ident[:, :])
                        last.then_inc(t_full, 1)
            pe.wait_ge(const_made, 6)
            pe.wait_ge(acc_free, 10)
            for v in range(4):
                pe.wait_ge(t_free, 21 + v)
                for b in range(4):
                    c = 4 * v + b
                    last = pe.transpose(trans[:, v % 2, b * P:(b + 1) * P], av_t[:, c * CHUNK:c * CHUNK + P], ident[:, :])
                last.then_inc(t_full, 1)

            with pe.Fori(0, HEADS) as h:
                def s_bank(key):
                    n = S_AT[key]
                    if n < S_RING:
                        pe.wait_ge(s_free_dve, h * len(S_BY_DVE))
                        pe.wait_ge(s_free_act, h * len(S_BY_ACT))
                    else:
                        last = S_UNITS[n - S_RING]
                        if last in S_BY_DVE:
                            pe.wait_ge(s_free_dve, at(S_BY_DVE[last], h, len(S_BY_DVE)))
                        else:
                            pe.wait_ge(s_free_act, at(S_BY_ACT[last], h, len(S_BY_ACT)))
                    return score[:, n % S_RING, :]

                def t_bank(step):
                    n = T_AT[step]
                    pe.wait_ge(t_free, at(n - T_RING, h, NTB, PRE_T))
                    return trans[:, n % T_RING, :]

                def o_bank(key):
                    n = O_AT[key]
                    pe.wait_ge(o_free, at(n - 1, h, NO) if n else h * NO)
                    return mixo[:, 0:MEM]

                def project_quarter(w, s, q):
                    if q == 0:
                        if s == 0:
                            pe.wait_ge(w_lo_done, at(w, h, NT, PRE_TILES))
                        pe.wait_ge(acc_free, at(2 * w + s - 2, h, 2 * NT, PRE_ACC))
                    for k in (2 * q, 2 * q + 1):
                        last = project(w, s, k)
                    if q == 3:
                        last.then_inc(acc_full, 1)

                def b_scores(i):
                    if i == 0:
                        pe.wait_ge(acc_free, at(3, h, 2 * NT, PRE_ACC))
                    rows_i = slice(i * P, (i + 1) * P)
                    for p, (a, n) in enumerate(b_pieces(i)):
                        for c in range(2):
                            out = s_bank(("b", i, p, c))[:, 0:n]
                            ps = slice(c * DK, (c + 1) * DK)
                            pe.matmul(out, q_b[:, c, rows_i], k_b[:, c, a:a + n], start=True, stop=False,
                                      skip_group_check=True)
                            pe.matmul(out, q_b[ps, c, rows_i], k_lo[ps, a:a + n], start=False, stop=True,
                                      skip_group_check=True).then_inc(s_full, 1)

                def v_spread(half):
                    if half == 0:
                        pe.wait_ge(acc_free, at(5, h, 2 * NT, PRE_ACC))
                    out = t_bank(("v_spread", half))
                    for j in range(4):
                        last = pe.transpose(out[:, j * P:(j + 1) * P], bv_t[:, (4 * half + j) * P:(4 * half + j + 1) * P],
                                            ident[:, :])
                    last.then_inc(t_full, 1)

                def b_spread(g, u):
                    if u == 0:
                        pe.wait_ge(b_ready, at(2 * g + 1, h, ST))
                    out = t_bank(("b_spread", g, u))
                    for j in range(2):
                        for i in range(2):
                            last = pe.transpose(out[:, (2 * j + i) * P:(2 * j + i + 1) * P],
                                                logits[:, i, 0, (2 * u + j) * P:(2 * u + j + 1) * P], ident[:, :])
                    last.then_inc(t_full, 1)

                def p_slot(step):
                    pe.wait_ge(t_free, at(T_AT[step], h, NTB, PRE_T))
                    return PT_AT[step] % PT_RING

                def b_mix(g, u):
                    if g == 0:
                        pe.wait_ge(t_free, at(T_AT[("v_spread", 1)], h, NTB, PRE_T))
                    out = o_bank(("b_mix", g)) if u == 0 else mixo[:, 0:MEM]
                    slot = p_slot(("b_spread", g, u))
                    for j in range(2):
                        cols = slice(j * MEM, (j + 1) * MEM)
                        last = product(out, v_hi[:, 2 * u + j, :], v_lo[:, 2 * u + j, :], p_hi[:, slot, cols],
                                       p_lo[:, slot, cols], u == 0 and j == 0, u == g and j == 1)
                    last.then_inc(pt_done, 1)

                def m_scores(m):
                    if m == 0:
                        pe.wait_ge(acc_free, at(11, h, 2 * NT, PRE_ACC))
                        pe.wait_ge(mkv_lo, h * 2 + 2)
                    out = s_bank(("m", m))
                    for i in range(2):
                        r = slice((2 * m + i) * P, (2 * m + i + 1) * P)
                        last = product(out[:, i * MEM:(i + 1) * MEM], q_m_hi[:, r], q_m_lo[:, r], mk_hi[:, :],
                                       mk_lo[:, :], True, True)
                    last.then_inc(s_full, 1)

                def m_spread(m):
                    pe.wait_ge(m_ready, at(m, h, 4))
                    out = t_bank(("m_spread", m))
                    for j in range(2):
                        for i in range(2):
                            last = pe.transpose(out[:, (2 * j + i) * P:(2 * j + i + 1) * P],
                                                m_probs[:, i, j * P:(j + 1) * P], ident[:, :])
                    last.then_inc(t_full, 1)

                def m_mix(m):
                    out = o_bank(("m_mix", m))
                    slot = p_slot(("m_spread", m))
                    for j in range(2):
                        cols = slice(j * MEM, (j + 1) * MEM)
                        last = product(out, mv_hi[:, j, :], mv_lo[:, j, :], p_hi[:, slot, cols],
                                       p_lo[:, slot, cols], j == 0, j == 1)
                    last.then_inc(pt_done, 1)

                def a_scores(m):
                    if m == 0:
                        pe.wait_ge(acc_free, at(7, h, 2 * NT, PRE_ACC))
                    outs = [s_bank(("a", m, g)) for g in range(2)]
                    for i in range(2):
                        t = 2 * m + i
                        for g in range(2):
                            ps = slice(g * DK, (g + 1) * DK)
                            last = pe.matmul(outs[g][:, i * MEM:i * MEM + 3 * CHUNK], a_q[ps, t * P:(t + 1) * P],
                                             a_k[ps, t * P:t * P + 3 * CHUNK], start=True, stop=True,
                                             skip_group_check=True)
                            if i == 1:
                                last.then_inc(s_full, 1)

                def a_spread(m):
                    pe.wait_ge(a_ready, at(m, h, 4))
                    out = t_bank(("a_spread", m))
                    for n in range(4):
                        last = pe.transpose(out[:, n * P:(n + 1) * P], a_probs[:, n, :], ident[:, :])
                    last.then_inc(t_full, 1)

                def a_mix(m):
                    out = o_bank(("a_mix", m))
                    pe.wait_ge(t_free, at(T_AT[("a_spread", m)], h, NTB, PRE_T))
                    for i in range(2):
                        for c in range(2):
                            chunk = 2 * (2 * m + i) + c
                            for g in range(2):
                                ps = slice(g * DK, (g + 1) * DK)
                                last = pe.matmul(out[ps, i * P + c * CHUNK:i * P + (c + 1) * CHUNK], a_v[:, chunk, ps],
                                                 a_pt[:, 2 * g + i, c * CHUNK:(c + 1) * CHUNK], start=True, stop=True,
                                                 skip_group_check=True)
                    last.then_inc(a_mixed, 1)

                def b_squares(s):
                    out = t_bank(("b_squares", s))
                    slot = PT_AT[("b_squares", s)] % PT_RING
                    pe.wait_ge(squares_split, at(s, h, 2))
                    pe.matmul(out, ones[:, :], p_hi[:, slot, :], start=True, stop=False, skip_group_check=True)
                    pe.matmul(out, ones[:, :], p_lo[:, slot, :], start=False, stop=True, skip_group_check=True)\
                      .then_inc(t_full, 1)

                for s in HEAD:
                    if s[0] == "project":
                        project_quarter(*s[1:])
                    elif s[0] == "b_scores":
                        b_scores(s[1])
                    elif s[0] == "v_spread":
                        v_spread(s[1])
                    elif s[0] == "b_spread":
                        b_spread(*s[1:])
                    elif s[0] == "b_mix":
                        b_mix(*s[1:])
                    elif s[0] == "m_scores":
                        m_scores(s[1])
                    elif s[0] == "m_spread":
                        m_spread(s[1])
                    elif s[0] == "m_mix":
                        m_mix(s[1])
                    elif s[0] == "a_scores":
                        a_scores(s[1])
                    elif s[0] == "a_spread":
                        a_spread(s[1])
                    elif s[0] == "a_mix":
                        a_mix(s[1])
                    elif s[0] == "b_squares":
                        b_squares(s[1])

            w_out_hi = [w_hi[:, 0, :]] + [wo[:, j, 0, :] for j in range(MIX_TILES - 1)]
            w_out_lo = [w_lo[:, 0, :]] + [wo[:, j, 1, :] for j in range(MIX_TILES - 1)]
            pe.wait_ge(acc_free, PRE_ACC + 2 * NT * HEADS)
            pe.wait_ge(s_free_dve, len(S_BY_DVE) * HEADS)
            pe.wait_ge(s_free_act, len(S_BY_ACT) * HEADS)
            with pe.Fori(0, ST // 2) as z:
                for par in range(2):
                    pe.wait_ge(y_added[par], z * 2)
                    for j in range(MIX_TILES):
                        pe.wait_ge(w_lo_done, PRE_TILES + NT * HEADS + j + 1)
                        if j in (0, 9):
                            pe.wait_ge(mix_lo_done, z * 4 + (2 * par + 1 + j // 9))
                        first, end = j == 0, j == MIX_TILES - 1
                        halves = [slice(0, HALF), slice(HALF, 2 * HALF)]
                        outs = y_acc[2 * par:2 * par + 2]
                        a_hi, a_lo = mix_hi[:, par, j, :], mix_lo[:, par, j, :]
                        for out, cols in zip(outs, halves):
                            pe.matmul(out, a_hi, w_out_hi[j][:, cols], start=first, stop=False, skip_group_check=True)
                        for out, cols in zip(outs, halves):
                            pe.matmul(out, a_hi, w_out_lo[j][:, cols], start=False, stop=False, skip_group_check=True)
                        for out, cols in zip(outs, halves):
                            last = pe.matmul(out, a_lo, w_out_hi[j][:, cols], start=False, stop=end,
                                             skip_group_check=True)
                    last.then_inc(y_full, 1)


_INS = ["x", "mem", "w_in", "g_norm", "a_sinks", "b_lambda_q1", "b_lambda_k1", "b_lambda_q2", "b_lambda_k2",
        "b_subln_g", "g_mem", "w_mem_kv", "w_out", "g_final"]


def kernel(**inputs):
    import numpy as np
    import concourse.bacc as bacc
    from concourse.bass_utils import run_bass_kernel_spmd

    nc = bacc.Bacc("TRN2", target_bir_lowering=False, num_devices=1)
    arrays, args = {}, []
    for name in _INS:
        a = np.ascontiguousarray(inputs[name])
        arrays[f"in_{name}"] = a
        args.append(nc.dram_tensor(f"in_{name}", a.shape, mybir.dt.from_np(a.dtype), kind="ExternalInput").ap())
    args.append(nc.dram_tensor("out_y", (1, SEQ, D), F32, kind="ExternalOutput").ap())
    build(nc, *args)
    r = run_bass_kernel_spmd(nc, [arrays], core_ids=[0])
    return r.results[0]["out_y"]
```

```python
import concourse.bass as bass
from concourse import mybir
from contextlib import ExitStack
from math import prod

F32 = mybir.dt.float32
F32R = mybir.dt.float32r
ALU = mybir.AluOpType
ACT = mybir.ActivationFunctionType
AX = mybir.AxisListType

P = 128
SEQ, D, MEM = 1024, 1024, 256
KT = D // P
ST = SEQ // P
HALF = 512
EPS = 1e-6
CHUNK = 64
HEADS = 4
DK = 64
AQ, AK, AV, AG, BQ, BK, BV, BG, MQ, MG = 0, 512, 640, 768, 1280, 1792, 2304, 2816, 3328, 3840
MIX_TILES = 12
POOL_WO = 2
LAM_INIT = 0.8 - 0.6
QK_SCALE = DK ** -0.5
M_SCALE = float(P) ** -0.5
MASKED = -1e30 * 2.0 ** 8

TILES = [("bk", BK, True), ("bq", BQ, True), ("bv", BV, False), ("aq", AQ, True),
         ("ag", AG, True), ("mq", MQ, False), ("mg", MG, False), ("bg", BG, False)]
NT = len(TILES)
BUSY = (32, 12, 16)
PRE_TILES = 10
PRE_ACC = 12
PRE_T = 26

BETWEEN = {
    (2, 0, 2): [("b_scores", 0, 0)],
    (2, 0, 3): [("b_scores", 1, 0), ("b_combine", 0)],
    (2, 1, 1): [("b_combine", 1)],
    (2, 1, 3): [("b_spread", 0, 0)],
    (3, 0, 0): [("b_scores", 2, 0)],
    (3, 0, 1): [("b_scores", 3, 0), ("b_combine", 2)],
    (3, 0, 2): [("b_combine", 3), ("v_spread", 0), ("v_spread", 1)],
    (3, 1, 2): [("b_spread", 1, 0), ("b_scores", 4, 0), ("b_spread", 1, 1), ("b_mix", 0, 0)],
    (4, 0, 0): [("b_scores", 4, 1), ("b_scores", 5, 0), ("b_mix", 1, 0), ("b_scores", 5, 1)],
    (4, 0, 2): [("b_combine", 4), ("a_scores", 0), ("b_combine", 5)],
    (4, 0, 3): [("a_norm", 0)],
    (4, 1, 2): [("b_mix", 1, 1), ("b_spread", 2, 0), ("b_spread", 2, 1)],
    (4, 1, 3): [("b_scores", 6, 0), ("b_spread", 2, 2), ("b_mix", 2, 0), ("b_mix", 2, 1), ("b_scores", 6, 1)],
    (5, 0, 0): [("b_scores", 7, 0), ("a_spread", 0), ("b_scores", 7, 1)],
    (5, 0, 1): [("a_scores", 1)],
    (5, 0, 2): [("b_combine", 6)],
    (5, 0, 3): [("b_combine", 7)],
    (5, 1, 1): [("a_norm", 1), ("b_mix", 2, 2)],
    (6, 0, 0): [("b_spread", 3, 0), ("b_spread", 3, 1), ("a_scores", 2), ("a_mix", 0), ("a_spread", 1), ("m_scores", 0), ("a_norm", 2)],
    (6, 0, 1): [("b_spread", 3, 2)],
    (6, 0, 2): [("b_mix", 3, 0), ("m_norm", 0)],
    (6, 0, 3): [("b_spread", 3, 3), ("b_mix", 3, 1)],
    (6, 1, 0): [("b_mix", 3, 2), ("m_spread", 0), ("b_mix", 3, 3), ("m_scores", 1)],
    (6, 1, 1): [("a_mix", 1), ("b_squares", 0), ("m_norm", 1), ("a_scores", 3), ("m_scores", 2), ("a_spread", 2)],
    (6, 1, 2): [("a_norm", 3), ("m_spread", 1), ("m_norm", 2), ("m_mix", 0)],
    (7, 0, 0): [("m_scores", 3)],
    (7, 0, 1): [("a_mix", 2), ("m_norm", 3), ("m_spread", 2)],
    (7, 0, 2): [("m_mix", 1)],
    (7, 0, 3): [("m_spread", 3), ("m_mix", 2)],
    (7, 1, 0): [("a_spread", 3), ("m_mix", 3), ("b_squares", 1)],
    (7, 1, 1): [("b_finish", 0)],
    (7, 1, 2): [("b_finish", 1)],
    (7, 1, 3): [("b_gate",), ("a_mix", 3)],
}




def head_steps():
    out = [("start",)]
    for w in range(NT):
        out.append(("weights", w + 1))
        for s in range(2):
            for q in range(4):
                out.append(("project", w, s, q))
                if q == 3:
                    out.append(("evacuate", w, s))
                out += BETWEEN.get((w, s, q), [])
    return out


HEAD = head_steps()


def b_pieces(i):
    width = 2 * P * (i // 2 + 1)
    return [(a, min(HALF, width - a)) for a in range(0, width, HALF)]


def numbered(*events):
    return {key: n for n, key in enumerate(events)}


def score_units():
    out = []
    for s in HEAD:
        if s[0] == "b_scores":
            out += [("b",) + s[1:] + (c,) for c in range(2)]
        if s[0] == "m_scores":
            out.append(("m", s[1]))
        if s[0] == "a_scores":
            out += [("a", s[1], g) for g in range(2)]
    return out


S_UNITS = score_units()
S_AT = numbered(*S_UNITS)
S_BY_DVE = numbered(*[u for u in S_UNITS if u[0] != "m"])
S_BY_ACT = numbered(*[u for u in S_UNITS if u[0] == "m"])
T_AT = numbered(*[s for s in HEAD if s[0] in ("v_spread", "b_spread", "m_spread", "a_spread", "b_squares")])
T_SPLIT = numbered(*[s for s in HEAD if s[0] in ("v_spread", "b_spread", "m_spread")])
PT_AT = numbered(*[s for s in HEAD if s[0] in ("b_spread", "m_spread", "b_squares")])
PT_MIX = numbered(*[s for s in HEAD if s[0] in ("b_spread", "m_spread")])
assert list(PT_MIX) == [(s[0][0] + "_spread",) + s[1:] for s in HEAD if s[0] in ("b_mix", "m_mix")]
O_AT = numbered(*[s[:2] for s in HEAD
                  if s[0] in ("m_mix", "a_mix") or (s[0] == "b_mix" and s[2] == s[1])])
NS, NTB, NPT, NO = len(S_AT), len(T_AT), len(PT_AT), len(O_AT)
S_RING, T_RING, PT_RING = 3, 2, 2
assert NS % S_RING == 0 and NTB % T_RING == 0 and NPT % PT_RING == 0 and PRE_T % T_RING == 0
NMIX = len(PT_MIX)


def build(nc, x, mem, w_in, g_norm, a_sinks, lq1, lk1, lq2, lk2, subln_g, g_mem, w_mem_kv, w_out,
          g_final, y):
    mixed = nc.dram_tensor("mixed", (MIX_TILES * P, SEQ), F32).ap()

    x_rows = x.rearrange("b (t p) d -> p (b t) d", p=P)
    y_rows = y.rearrange("b (t p) d -> p (b t) d", p=P)
    mem_rows = mem.rearrange("b (t p) d -> p (b t) d", p=P)
    w_in_v = w_in.rearrange("l (k p) n -> p (l k) n", p=P)
    w_mem_v = w_mem_kv.rearrange("l (k p) n -> p (l k) n", p=P)
    w_out_v = w_out.rearrange("l m n -> (l m) n")
    mixed_v = mixed.rearrange("(j p) s -> p j s", p=P)

    place = [(nc.sbuf_base + 63) // 64 * 64]
    begins = {}

    def sb(name, shape, dt=F32):
        begins[name] = place[0]
        t = nc.alloc_sbuf_tensor_at(name, shape, dt, offset=place[0])
        place[0] += (prod(shape[1:]) * 4 + 31) // 32 * 32
        return t

    def sb_over(name, shape, begin, end, dt=F32):
        assert begin + prod(shape[1:]) * 4 <= end, (name, begin, end)
        return nc.alloc_sbuf_tensor_at(name, shape, dt, offset=begin)

    ctx = ExitStack()
    with ctx:
        def sem(name):
            return ctx.enter_context(nc.semaphore(name))

        w_raw = sb("w_raw", [P, 2, KT * P])
        w_hi = sb("w_hi", [P, 2, KT * P], F32R)
        w_lo = sb("w_lo", [P, 2, KT * P], F32R)
        gates = {g: sb(f"gate_{g}", [P, SEQ]) for g in "abm"}
        ident = sb("ident", [P, P])
        ones = sb("ones", [P, P], F32R)
        small = sb("small", [P, 64])
        eps = small[:, 0:1]
        neg_lam = small[:, 1:2]
        subln = small[:, 2:3]
        lam_sums = small[:, 4:6]
        lam_exps = small[:, 6:8]
        ssq = small[:, 8:10]
        std = small[:, 10:12]
        rstd = small[:, 12:14]
        mean_sq = small[:, 40:42]
        newton = small[:, 42:44]
        newton_by = small[:, 44:46]
        rstd_fine = small[:, 46:48]
        y_ssq = small[:, 48:52]
        sink_in = small[:, 16:24]
        sinks = small[:, 24:40]
        stats_b = sb("stats_b", [P, 32])
        b_max = stats_b[:, 0:4]
        b_neg = stats_b[:, 4:8]
        b_sum = stats_b[:, 8:12]
        b_inv = stats_b[:, 12:16]
        stats_m = sb("stats_m", [P, 8])
        m_max, m_neg, m_sum, m_inv = (stats_m[:, 2 * n:2 * n + 2] for n in range(4))
        stats_a = sb("stats_a", [P, 32])
        a_max, a_top, a_neg, a_off, a_exp, a_sum, a_den, a_inv = (stats_a[:, 4 * n:4 * n + 4] for n in range(8))

        q_b = sb("q_b", [P, 2, SEQ], F32R)
        k_b = sb("k_b", [P, 2, SEQ], F32R)
        k_lo = sb("k_lo", [P, SEQ], F32R)
        v_hi = sb("v_hi", [P, ST, P], F32R)
        v_lo = sb("v_lo", [P, ST, P], F32R)
        x_hi = sb("x_hi", [P, KT, SEQ], F32R)
        x_lo = sb("x_lo", [P, KT, SEQ], F32R)
        logits = sb("logits", [P, 2, 2, SEQ])
        p_hi = sb("p_hi", [P, PT_RING, HALF], F32R)
        p_lo = sb("p_lo", [P, PT_RING, HALF], F32R)
        mk_raw = sb("mk_raw", [P, HEADS, MEM])
        mv_raw = sb("mv_raw", [P, HEADS, 2, P])
        mk_hi = sb("mk_hi", [P, MEM], F32R)
        mk_lo = sb("mk_lo", [P, MEM], F32R)
        mv_hi = sb("mv_hi", [P, 2, P], F32R)
        mv_lo = sb("mv_lo", [P, 2, P], F32R)
        m_probs = sb("m_probs", [P, 2, MEM])
        a_q = sb("a_q", [P, SEQ])
        a_k = sb("a_k", [P, CHUNK + SEQ])
        a_v = sb("a_v", [P, 2 * ST, P])
        a_band = sb("a_band", [P, 4, P])
        a_probs = sb("a_probs", [P, 4, P])
        a_pt = sb("a_pt", [P, 4, P])
        b_out = sb("b_out", [P, CHUNK + SEQ])
        b_bias = sb("b_bias", [P, SEQ + P])
        a_bias = sb("a_bias", [P, 2, 2, P])
        main_end = place[0]
        q_m_hi, q_m_lo = q_b[:, 0, :], q_b[:, 1, :]
        bv_t = b_out[:, 0:SEQ]
        squares = logits[:, 0, 0, :]
        inv_rms = logits[:, 0, 1, :]
        mem_hi = q_b[:, :, :].rearrange("p a n -> p (a n)").rearrange("p (k n) -> p k n", k=KT)
        mem_lo = k_b[:, :, :].rearrange("p a n -> p (a n)").rearrange("p (k n) -> p k n", k=KT)
        mem_raw = [sb_over(f"mem_raw{n}", [P, D], begins["p_hi"] + n * D * 4, begins["mk_raw"]) for n in range(2)]
        rows_raw = [logits[:, 0, 0, :], logits[:, 0, 1, :]]
        rows = [logits[:, 1, 0, :], logits[:, 1, 1, :]]
        g_norm_b, g_mem_b, mv_t = gates["a"], gates["b"], gates["m"]
        av_t = b_out
        lam_in = a_pt[:, :, 0:DK]
        lam_prod = a_band[:, 0:2, 0:DK]

        WO = 2 * D * 4
        wo_begins = [begins["k_b"], begins["q_b"], begins["k_lo"]]
        wo_begins += [begins["x_hi"] + n * WO for n in range(2 * KT * SEQ * 4 // WO)]
        wo = [sb_over(f"wo{j + 1}", [P, 2, D], b, b + WO, F32R)
              for j, b in enumerate(wo_begins[:MIX_TILES - 1])]
        wo_raw = [sb_over(f"wo_raw{j + 1}", [P, D], b + D * 4, b + WO)
                  for j, b in enumerate(wo_begins[:MIX_TILES - 1])]
        MIX = MIX_TILES * P * 4
        spread_end = begins["mk_raw"] + 2 * HEADS * MEM * 4
        mix_raw = [sb_over("mix_raw0", [P, MIX_TILES, P], spread_end - MIX, spread_end),
                   sb_over("mix_raw1", [P, MIX_TILES, P], begins["b_bias"], main_end)]
        mix_hi = [sb_over("mix_hi0", [P, MIX_TILES, P], main_end, nc.sbuf_usable_end, F32R),
                  sb_over("mix_hi1", [P, MIX_TILES, P], begins["logits"] + 2 * SEQ * 4, begins["p_hi"], F32R)]
        mix_lo_begin = begins["logits"] + 2 * SEQ * 4 + MIX
        mix_lo = [sb_over(f"mix_lo{n}", [P, MIX_TILES, P], mix_lo_begin + n * MIX, spread_end - MIX, F32R)
                  for n in range(2)]
        rows_begin = begins["mk_hi"]
        x_res = sb_over("x_res", [P, 2, D], rows_begin, begins["b_out"])
        y_row = sb_over("y_row", [P, 2, D], rows_begin + 2 * D * 4, begins["b_out"])
        y_sq = sb_over("y_sq", [P, D], rows_begin + 4 * D * 4, begins["b_out"])
        g_fin = sb_over("g_fin", [P, D], rows_begin + 5 * D * 4, begins["b_out"])
        assert main_end <= nc.sbuf_usable_end, main_end

        acc = ctx.enter_context(nc.psum_tensor("acc", [P, 2, HALF], F32))
        score = ctx.enter_context(nc.psum_tensor("score", [P, S_RING, HALF], F32))
        trans = ctx.enter_context(nc.psum_tensor("trans", [P, T_RING, HALF], F32))
        mixo = ctx.enter_context(nc.psum_tensor("mixo", [P, HALF], F32))
        y_acc = [score[:, 0, :], score[:, 1, :], trans[:, 0, :], trans[:, 1, :]]

        raw_full = [sem("raw_full0"), sem("raw_full1")]
        w_hi_done = sem("w_hi_done")
        w_lo_done = sem("w_lo_done")
        mem_full = [sem("mem_full0"), sem("mem_full1")]
        rows_full = [sem("rows_full0"), sem("rows_full1")]
        consts_full = sem("consts_full")
        gmem_full = sem("gmem_full")
        gnorm_full = sem("gnorm_full")
        rows_std = sem("rows_std")
        rows_sq = sem("rows_sq")
        mean_made = sem("mean_made")
        rows_inv = sem("rows_inv")
        rows_done = sem("rows_done")
        acc_full = sem("acc_full")
        acc_part = sem("acc_part")
        acc_free = sem("acc_free")
        t_full = sem("t_full")
        t_hi = sem("t_hi")
        t_free = sem("t_free")
        s_full = sem("s_full")
        s_free_dve = sem("s_free_dve")
        s_free_act = sem("s_free_act")
        pt_done = sem("pt_done")
        squares_split = sem("squares_split")
        squares_made = sem("squares_made")
        squares_hi = sem("squares_hi")
        a_mixed = sem("a_mixed")
        o_free = sem("o_free")
        bias_made = sem("bias_made")
        b_neg_made = sem("b_neg_made")
        b_exp = sem("b_exp")
        b_inv_made = sem("b_inv_made")
        b_scaled = sem("b_scaled")
        b_ready = sem("b_ready")
        m_max_made = sem("m_max_made")
        m_neg_made = sem("m_neg_made")
        m_inv_made = sem("m_inv_made")
        m_ready = sem("m_ready")
        mkv_hi = sem("mkv_hi")
        mkv_lo = sem("mkv_lo")
        a_max_made = sem("a_max_made")
        a_top_made = sem("a_top_made")
        a_neg_made = sem("a_neg_made")
        a_off_made = sem("a_off_made")
        a_exp_made = sem("a_exp_made")
        a_den_made = sem("a_den_made")
        a_inv_made = sem("a_inv_made")
        a_ready = sem("a_ready")
        rms_made = sem("rms_made")
        inv_made = sem("inv_made")
        b_normed = sem("b_normed")
        b_gated = sem("b_gated")
        spilled = {g: sem(f"spilled_{g}") for g in "abm"}
        mask_made = sem("mask_made")
        const_made = sem("const_made")
        table_step = sem("table_step")
        lam_exp = sem("lam_exp")
        mix_full = [sem("mix_full0"), sem("mix_full1")]
        mix_last = [sem("mix_last0"), sem("mix_last1")]
        wo_full = [sem(f"wo_full{j}") for j in range(1, MIX_TILES)]
        wo_hi_done = sem("wo_hi_done")
        wo_lo_first = sem("wo_lo_first")
        wo_lo_done = sem("wo_lo_done")
        mix_lo_mid = sem("mix_lo_mid")
        mix_hi_done = sem("mix_hi_done")
        mix_lo_done = sem("mix_lo_done")
        y_full = sem("y_full")
        res_full = [sem("res_full0"), sem("res_full1")]
        gfin_full = sem("gfin_full")
        y_added = [sem("y_added0"), sem("y_added1")]
        y_sqd = sem("y_sqd")
        y_sum = sem("y_sum")
        y_std = sem("y_std")
        y_inv = sem("y_inv")
        y_done = sem("y_done")
        stored = [sem("stored0"), sem("stored1")]

        block = ctx.enter_context(nc.Block())

        def at(number, h, per_turn, before=0):
            return h * per_turn + (before + number + 1)

        def raw_at(w, h):
            return h * (NT // 2 * 32) + 32 * ((PRE_TILES + w) // 2 + 1)

        @block.sync
        def _(sp):
            def load_tile(view, slot, cols, split):
                dst = w_raw[:, slot, :].rearrange("p (k n) -> p k n", k=KT)
                if split is not None:
                    for c in range(2):
                        sp.dma_start(dst[:, :, c * DK:(c + 1) * DK], view[:, :, bass.ds(cols + c * split, DK)])\
                          .then_inc(raw_full[slot], 16)
                else:
                    for c in range(2):
                        ks = slice(c * KT // 2, (c + 1) * KT // 2)
                        sp.dma_start(dst[:, ks, :], view[:, ks, bass.ds(cols, P)]).then_inc(raw_full[slot], 16)

            sp.dma_start(mem_raw[0][:, :], mem_rows[:, 0, :]).then_inc(mem_full[0], 16)
            sp.dma_start(g_mem_b[:, :], g_mem.partition_broadcast(P)[:, 0, :]).then_inc(gmem_full, 16)
            sp.dma_start(mem_raw[1][:, :], mem_rows[:, 1, :]).then_inc(mem_full[1], 16)
            load_tile(w_mem_v, 0, 0, None)
            sp.dma_start(rows_raw[0], x_rows[:, 0, :]).then_inc(rows_full[0], 16)
            sp.dma_start(g_norm_b[:, :], g_norm.partition_broadcast(P)[:, 0, :]).then_inc(gnorm_full, 16)
            load_tile(w_mem_v, 1, 4 * P, None)
            sp.dma_start(rows_raw[1], x_rows[:, 1, :]).then_inc(rows_full[1], 16)
            for j, v in enumerate((lq1, lk1, lq2, lk2)):
                sp.dma_start(lam_in[:, j, :], v.partition_broadcast(P)[:, 0, :]).then_inc(consts_full, 16)
            sp.dma_start(sink_in, a_sinks.partition_broadcast(P)[:, 0, :]).then_inc(consts_full, 16)
            sp.dma_start(subln, subln_g.rearrange("l p -> p l")).then_inc(consts_full, 16)
            with sp.Fori(0, 3) as q:
                for par in range(2):
                    sp.wait_ge(w_lo_done, q * 2 + par + 1)
                    load_tile(w_mem_v, par, q * P + (P + 4 * P * par), None)
                    sp.wait_ge(rows_done, q * 2 + par + 3)
                    row = x_rows[:, bass.ds(q * 2 + (par + 2), 1), :].rearrange("p a n -> p (a n)")
                    sp.dma_start(rows_raw[par], row)\
                      .then_inc(rows_full[par], 16)
            for par, col in enumerate((AV, AK)):
                sp.wait_ge(w_lo_done, 7 + par)
                load_tile(w_in_v, par, col, None)
            for w in range(2):
                sp.wait_ge(w_lo_done, PRE_TILES - 1 + w)
                load_tile(w_in_v, w, TILES[w][1], 4 * DK)

            def load_head_tile(w, h):
                name, col, two = TILES[w % NT]
                step = DK if two else P
                sp.wait_ge(w_lo_done, at(w - 2, h, NT, PRE_TILES))
                load_tile(w_in_v, w % 2, h * step + (col + (step if w >= NT else 0)), 4 * DK if two else None)

            def spill(g, h):
                if g == "b":
                    sp.wait_ge(b_gated, h * 2 + 2)
                else:
                    sp.wait_ge(o_free, at(O_AT[(f"{g}_mix", 3)], h, NO))
                sp.dma_start(mixed_v[:, bass.ds(h * 3 + "abm".index(g), 1), :],
                             gates[g][:, :].rearrange("p (a n) -> p a n", a=1)).then_inc(spilled[g], 16)

            with sp.Fori(0, HEADS - 1) as h:
                for w in range(2, NT + 2):
                    load_head_tile(w, h)
                for g in "amb":
                    spill(g, h)
            for w in range(2, NT):
                load_head_tile(w, HEADS - 1)

            n_tiles = PRE_TILES + NT * HEADS

            def load_wo(j):
                t, g = divmod(j, 3)
                first = (t * DK, (512 + t * P), (1024 + t * P))[g]
                second = first + (4 * DK if g == 0 else DK)
                dst = wo_raw[j - 1] if j else w_raw[:, 0, :]
                for c, row in enumerate((first, second)):
                    sp.dma_start(dst[c * DK:(c + 1) * DK, :], w_out_v[row:row + DK, :])\
                      .then_inc(wo_full[j - 1] if j else raw_full[0], 16)

            def load_mix(par, t, part):
                js, done = ((slice(0, 9), mix_full), (slice(9, 12), mix_last))[part]
                sp.dma_start(mix_raw[par][:, js, :], mixed_v[:, js, bass.ds(t * P, P)]).then_inc(done[par], 16)

            def load_residual(par, t):
                sp.dma_start(x_res[:, par:par + 1, :], x_rows[:, bass.ds(t, 1), :]).then_inc(res_full[par], 16)

            H = HEADS - 1
            sp.wait_ge(w_lo_done, n_tiles - 1)
            load_wo(0)
            for g in "abm":
                sp.wait_ge(spilled[g], 16 * H)
            sp.wait_ge(mkv_lo, 2 * HEADS)
            load_mix(0, 0, 0)
            sp.wait_ge(s_full, at(S_AT[("b", 7, 1, 1)], H, NS))
            load_wo(1)
            sp.wait_ge(s_free_dve, len(S_BY_DVE) * HEADS)
            load_mix(1, 1, 0)
            sp.wait_ge(s_full, NS * HEADS)
            load_wo(2)
            sp.wait_ge(pt_done, at(PT_MIX[("b_spread", 3, 3)], H, NMIX))
            load_wo(3)
            sp.wait_ge(acc_full, PRE_ACC + 2 * NT * HEADS)
            for j in range(4, 8):
                load_wo(j)
            for g in "mab":
                spill(g, H)
            load_wo(8)
            load_wo(9)
            for g in "mab":
                sp.wait_ge(spilled[g], 16 * HEADS)
            load_mix(0, 0, 1)
            load_mix(1, 1, 1)
            for j in range(10, MIX_TILES):
                load_wo(j)
            sp.wait_ge(t_free, PRE_T + NTB * HEADS)
            sp.wait_ge(pt_done, NMIX * HEADS)
            sp.wait_ge(a_mixed, 4 * HEADS)
            load_residual(0, 0)
            load_residual(1, 1)
            sp.dma_start(g_fin[:, :], g_final.partition_broadcast(P)).then_inc(gfin_full, 16)

            def store(par, z):
                for s in range(2):
                    cols = slice(s * HALF, (s + 1) * HALF)
                    sp.wait_ge(y_done, z * 4 + (2 * par + s + 1))
                    sp.dma_start(y_rows[:, bass.ds(z * 2 + par, 1), cols], y_row[:, par:par + 1, cols])\
                      .then_inc(stored[par], 16)

            def next_pair(z, split):
                for par in range(2):
                    sp.wait_ge(mix_lo_done, split[par])
                    for part in range(2):
                        load_mix(par, z * 2 + (par + 2), part)
                for par in range(2):
                    sp.wait_ge(y_added[par], z * 2 + 2)
                    load_residual(par, z * 2 + (par + 2))
                    store(par, z)

            sp.wait_ge(mix_lo_mid, 1)
            next_pair(0, (4, 5))
            with sp.Fori(0, ST // 2 - 2) as n:
                next_pair(n + 1, (n * 4 + 7, n * 4 + 9))
            for par in range(2):
                store(par, ST // 2 - 1)
            for par in range(2):
                sp.wait_ge(stored[par], 16 * ST)

        @block.scalar
        def _(act):
            def take_w_hi(slot):
                for s in range(2):
                    cols = slice(s * HALF, (s + 1) * HALF)
                    act.activation(w_hi[:, slot, cols], w_raw[:, slot, cols], ACT.Copy).then_inc(w_hi_done, 1)

            def split_hi(n):
                slot = n % 2
                act.wait_ge(raw_full[slot], 32 * (n // 2 + 1))
                if n >= 2:
                    act.wait_ge(acc_full, n - 1 if n < PRE_TILES else n)
                take_w_hi(slot)

            def row_stats(raw, par, full, done_before, r):
                act.wait_ge(*full)
                if done_before is not None:
                    act.wait_ge(t_full, done_before)
                act.activation(rows[par], raw[par][:, 0:D], ACT.Square, accum_out=ssq[:, par:par + 1])\
                   .then_inc(rows_sq, 1)
                act.wait_ge(rows_sq, r + 1)
                act.activation(std[:, par:par + 1], ssq[:, par:par + 1], ACT.Sqrt, bias=eps, scale=1.0 / D)\
                   .then_inc(rows_std, 1)

            act.wait_ge(const_made, 1)
            act.activation(std[:, 0:1], eps, ACT.Sqrt)
            for par in range(2):
                row_stats(mem_raw, par, (mem_full[par], 16), None, par)
            split_hi(0)
            for par in range(2):
                for u in range(2):
                    act.wait_ge(t_full, 2 * par + u + 1)
                    act.activation(mem_hi[:, 4 * u:4 * u + 4, par * P:(par + 1) * P],
                                   trans[:, u, :].rearrange("p (k n) -> p k n", k=4), ACT.Copy).then_inc(t_hi, 1)
            row_stats(rows_raw, 0, (rows_full[0], 16), 2, 2)

            def prologue_step(q, par, more=True):
                n = 1 - par
                act.wait_ge(raw_full[n], (q * 32 + 32) if par == 0 else (q * 32 + 64))
                act.wait_ge(acc_full, q * 2 + par)
                take_w_hi(n)
                if more:
                    row_stats(rows_raw, n, (rows_full[n], q * 16 + (16 + 16 * par)), q * 4 + (4 + 2 * par),
                              q * 2 + (par + 3))
                for u in range(2):
                    act.wait_ge(t_full, q * 4 + (5 + 2 * par + u))
                    act.activation(x_hi[:, 4 * u:4 * u + 4, bass.ds(q * 2 * P + par * P, P)],
                                   trans[:, u, :].rearrange("p (k n) -> p k n", k=4), ACT.Copy)\
                       .then_inc(t_hi, 1)

            with act.Fori(0, 3) as q:
                for par in range(2):
                    prologue_step(q, par)
            prologue_step(3, 0)
            prologue_step(3, 1, more=False)
            act.wait_ge(table_step, 2)
            act.activation(lam_exps, lam_sums, ACT.Exp).then_inc(lam_exp, 1)
            split_hi(9)
            split_hi(10)

            with act.Fori(0, HEADS) as h:
                def start():
                    act.wait_ge(t_free, 22)
                    act.wait_ge(s_full, h * NS)
                    act.wait_ge(pt_done, h * NMIX)
                    act.activation(mk_hi[:, :], mk_raw[:, bass.ds(h, 1), :].rearrange("p a n -> p (a n)"), ACT.Copy)\
                       .then_inc(mkv_hi, 1)
                    act.activation(mv_hi[:, :, :].rearrange("p a n -> p (a n)"),
                                   mv_raw[:, bass.ds(h, 1), :, :].rearrange("p h a n -> p (h a n)"), ACT.Copy)\
                       .then_inc(mkv_hi, 1)

                def weights(w):
                    slot = w % 2
                    act.wait_ge(raw_full[slot], raw_at(w, h))
                    act.wait_ge(acc_full, at(2 * w - 3, h, 2 * NT, PRE_ACC))
                    take_w_hi(slot)

                def evacuate(w, s):
                    name = TILES[w][0]
                    cols = slice(s * HALF, (s + 1) * HALF)
                    if name in ("bv", "aq"):
                        return
                    act.wait_ge(acc_full, at(2 * w + s, h, 2 * NT, PRE_ACC))
                    if name == "bk":
                        for c in range(2):
                            for half in range(2):
                                act.activation(k_b[half * DK:(half + 1) * DK, c, cols],
                                               acc[c * DK:(c + 1) * DK, s, :], ACT.Copy).then_inc(acc_part, 1)
                    elif name == "bq":
                        for c in range(2):
                            act.activation(q_b[c * DK:(c + 1) * DK, c, cols], acc[c * DK:(c + 1) * DK, s, :],
                                           ACT.Copy, scale=QK_SCALE).then_inc(acc_part, 1)
                    elif name == "mq":
                        act.wait_ge(s_full, at(S_AT[("b", 7, 1, 1)], h, NS))
                        act.activation(q_m_hi[:, cols], acc[:, s, :], ACT.Copy).then_inc(acc_part, 1)
                    else:
                        g = name[0]
                        act.wait_ge(spilled[g], h * 16)
                        act.activation(gates[g][:, cols], acc[:, s, :], ACT.Tanh, scale=0.5).then_inc(acc_part, 1)

                def b_scores(i, p):
                    if p < len(b_pieces(i)) - 1:
                        return
                    width = sum(n for _, n in b_pieces(i))
                    act.wait_ge(b_neg_made, at(i, h, ST))
                    for c in range(2):
                        act.activation(logits[:, i % 2, c, 0:width], logits[:, i % 2, c, 0:width], ACT.Exp,
                                       bias=b_neg[:, 2 * (i % 2) + c:2 * (i % 2) + c + 1],
                                       accum_out=b_sum[:, 2 * (i % 2) + c:2 * (i % 2) + c + 1])\
                           .then_inc(b_exp, 1)

                def take_hi(step, out):
                    bank = T_AT[step] % T_RING
                    act.wait_ge(t_full, at(T_AT[step], h, NTB, PRE_T))
                    act.activation(out, trans[:, bank, :], ACT.Copy).then_inc(t_hi, 1)

                def v_spread(half):
                    if half == 0:
                        act.wait_ge(pt_done, h * NMIX)
                    take_hi(("v_spread", half), v_hi[:, 4 * half:4 * half + 4, :].rearrange("p j n -> p (j n)"))

                def p_slot_free(n):
                    if n < PT_RING:
                        act.wait_ge(pt_done, h * NMIX)
                        act.wait_ge(t_full, h * NTB + PRE_T)
                        return
                    last = list(PT_AT)[n - PT_RING]
                    if last in PT_MIX:
                        act.wait_ge(pt_done, at(PT_MIX[last], h, NMIX))
                    else:
                        act.wait_ge(t_full, at(T_AT[last], h, NTB, PRE_T))

                def p_spread(step):
                    n = PT_AT[step]
                    p_slot_free(n)
                    take_hi(step, p_hi[:, n % PT_RING, :])

                def m_norm(m):
                    act.wait_ge(m_neg_made, at(m, h, 4))
                    bank = S_AT[("m", m)] % S_RING
                    if m > 0:
                        act.wait_ge(t_full, at(T_AT[("m_spread", m - 1)], h, NTB, PRE_T))
                    else:
                        act.wait_ge(t_full, h * NTB + PRE_T)
                    act.activation(m_probs[:, 0, :], score[:, bank, 0:MEM], ACT.Exp, bias=m_neg[:, 0:1],
                                   scale=M_SCALE, accum_out=m_sum[:, 0:1])
                    act.activation(m_probs[:, 1, :], score[:, bank, MEM:2 * MEM], ACT.Exp, bias=m_neg[:, 1:2],
                                   scale=M_SCALE, accum_out=m_sum[:, 1:2]).then_inc(s_free_act, 1)

                def a_scores(m):
                    act.wait_ge(a_off_made, at(m, h, 4))
                    for n in range(4):
                        act.activation(a_band[:, n, :], a_band[:, n, :], ACT.Exp, bias=a_neg[:, n:n + 1],
                                       accum_out=a_sum[:, n:n + 1])
                    act.activation(a_exp, a_off, ACT.Exp).then_inc(a_exp_made, 1)

                def b_squares(s):
                    n = PT_AT[("b_squares", s)]
                    act.wait_ge(squares_made, at(s, h, 2))
                    p_slot_free(n)
                    act.activation(p_hi[:, n % PT_RING, :], squares[:, s * HALF:(s + 1) * HALF], ACT.Copy)\
                       .then_inc(squares_hi, 1)

                def b_finish(s):
                    cols = slice(s * HALF, (s + 1) * HALF)
                    act.wait_ge(t_free, at(T_AT[("b_squares", s)], h, NTB, PRE_T))
                    act.activation(inv_rms[:, cols], inv_rms[:, cols], ACT.Sqrt).then_inc(rms_made, 1)

                for s in HEAD:
                    if s[0] == "start":
                        start()
                    elif s[0] == "weights":
                        weights(s[1])
                    elif s[0] == "evacuate":
                        evacuate(*s[1:])
                    elif s[0] == "b_scores":
                        b_scores(*s[1:])
                    elif s[0] in ("b_spread", "m_spread"):
                        p_spread(s)
                    elif s[0] == "v_spread":
                        v_spread(s[1])
                    elif s[0] == "m_norm":
                        m_norm(s[1])
                    elif s[0] == "a_scores":
                        a_scores(s[1])
                    elif s[0] == "b_squares":
                        b_squares(s[1])
                    elif s[0] == "b_finish":
                        b_finish(s[1])

            def mix_hi_part(par, js, arrived, full):
                act.wait_ge(arrived[par], full)
                act.activation(mix_hi[par][:, js, :], mix_raw[par][:, js, :], ACT.Copy).then_inc(mix_hi_done, 1)

            def wo_hi_part(j):
                act.wait_ge(wo_full[j - 1], 32)
                act.activation(wo[j - 1][:, 0, :], wo_raw[j - 1][:, :], ACT.Copy).then_inc(wo_hi_done, 1)

            mix_hi_part(0, slice(0, 3), mix_full, 16)
            act.wait_ge(t_full, at(T_AT[("b_spread", 3, 3)], HEADS - 1, NTB, PRE_T))
            mix_hi_part(1, slice(0, 3), mix_full, 16)
            wo_hi_part(1)
            wo_hi_part(2)
            mix_hi_part(0, slice(3, 9), mix_full, 16)
            mix_hi_part(1, slice(3, 9), mix_full, 16)
            for j in range(3, 7):
                wo_hi_part(j)
            mix_hi_part(0, slice(9, 12), mix_last, 16)
            mix_hi_part(1, slice(9, 12), mix_last, 16)
            for j in range(7, MIX_TILES):
                wo_hi_part(j)

            def finish_row(par, z):
                for s in range(2):
                    cols = slice(s * HALF, (s + 1) * HALF)
                    act.wait_ge(y_added[par], z * 2 + (s + 1))
                    act.activation(y_sq[:, cols], y_row[:, par, cols], ACT.Square,
                                   accum_out=y_ssq[:, 2 * par + s:2 * par + s + 1]).then_inc(y_sqd, 1)
                act.wait_ge(y_sum, z * 2 + (par + 1))
                act.activation(std[:, par:par + 1], ssq[:, par:par + 1], ACT.Sqrt, bias=eps, scale=1.0 / D)\
                   .then_inc(y_std, 1)

            with act.Fori(0, ST // 2 - 1) as z:
                for par in range(2):
                    act.wait_ge(y_full, z * 4 + 2 * (par + 1))
                    mix_hi_part(par, slice(0, 9), mix_full, z * 16 + 32)
                    mix_hi_part(par, slice(9, 12), mix_last, z * 16 + 32)
                    finish_row(par, z)
            for par in range(2):
                finish_row(par, ST // 2 - 1)

        @block.gpsimd
        def _(pool):
            pool.memset(eps, EPS).then_inc(const_made, 1)
            pool.memset(ident[:, :], 0.0).then_inc(mask_made, 1)
            pool.wait_ge(mask_made, 1)
            pool.affine_select(out=ident[:, :], in_=ident[:, :], compare_op=ALU.not_equal, fill=1.0,
                               base=0, pattern=[[-1, P]], channel_multiplier=1).then_inc(const_made, 1)
            pool.memset(a_k[:, 0:CHUNK], 0.0).then_inc(const_made, 1)
            pool.iota(b_bias[:, :], [[1, SEQ + P]], base=-(SEQ - P), channel_multiplier=-1,
                      allow_small_or_imprecise_dtypes=True).then_inc(const_made, 1)
            pool.iota(a_bias[:, :, :, :], [[0, 4], [1, P]], base=-CHUNK, channel_multiplier=-1,
                      allow_small_or_imprecise_dtypes=True).then_inc(const_made, 1)

            def split_lo(slot, n):
                for s in range(2):
                    cols = slice(s * HALF, (s + 1) * HALF)
                    pool.wait_ge(w_hi_done, n + (s + 1))
                    last = pool.tensor_tensor(w_lo[:, slot, cols], w_raw[:, slot, cols],
                                              w_hi[:, slot, cols].bitcast(F32), ALU.subtract)
                last.then_inc(w_lo_done, 1)

            pool.memset(av_t[:, 0:CHUNK], 0.0).then_inc(const_made, 1)
            split_lo(0, 0)
            with pool.Fori(0, 4) as q:
                for par in range(2):
                    split_lo(1 - par, q * 4 + 2 * (1 + par))
            split_lo(1, 2 * 9)
            split_lo(0, 2 * 10)

            with pool.Fori(0, HEADS) as h:
                def start():
                    pool.wait_ge(mkv_hi, h * 2 + 2)
                    pool.tensor_tensor(mk_lo[:, :], mk_raw[:, bass.ds(h, 1), :].rearrange("p a n -> p (a n)"),
                                       mk_hi[:, :].bitcast(F32), ALU.subtract).then_inc(mkv_lo, 1)
                    pool.tensor_tensor(mv_lo[:, :, :].rearrange("p a n -> p (a n)"),
                                       mv_raw[:, bass.ds(h, 1), :, :].rearrange("p h a n -> p (h a n)"),
                                       mv_hi[:, :, :].rearrange("p a n -> p (a n)").bitcast(F32), ALU.subtract)\
                        .then_inc(mkv_lo, 1)

                def b_combine(i):
                    width = sum(n for _, n in b_pieces(i))
                    pool.wait_ge(b_inv_made, at(i, h, ST))
                    pool.nop(nofuse=True)
                    pool.tensor_scalar(logits[:, i % 2, 1, 0:width], logits[:, i % 2, 1, 0:width],
                                       b_inv[:, 2 * (i % 2) + 1:2 * (i % 2) + 2], neg_lam, ALU.mult, ALU.mult)\
                        .then_inc(b_scaled, 1)

                def m_norm(m):
                    pool.wait_ge(m_inv_made, at(m, h, 4))
                    pool.tensor_tensor(m_probs[:, :, :], m_probs[:, :, :],
                                       m_inv.rearrange("p (a n) -> p a n", n=1).broadcast_to([P, 2, MEM]), ALU.mult)\
                        .then_inc(m_ready, 1)

                def a_norm(m):
                    pool.wait_ge(a_inv_made, at(m, h, 4))
                    if m > 0:
                        pool.wait_ge(t_full, at(T_AT[("a_spread", m - 1)], h, NTB, PRE_T))
                    else:
                        pool.wait_ge(t_full, h * NTB + PRE_T)
                    pool.tensor_tensor(a_probs[:, :, :], a_band[:, :, :],
                                       a_inv.rearrange("p (a n) -> p a n", n=1).broadcast_to([P, 4, P]), ALU.mult)\
                        .then_inc(a_ready, 1)

                def b_squares(s):
                    cols = slice(s * HALF, (s + 1) * HALF)
                    n = PT_AT[("b_squares", s)]
                    pool.wait_ge(o_free, at(O_AT[("b_mix", 2 * s + 1)], h, NO))
                    pool.wait_ge(t_full, at(T_AT[("b_spread", 3, 3)], h, NTB, PRE_T))
                    pool.tensor_tensor(squares[:, cols], b_out[:, cols], b_out[:, cols], ALU.mult)\
                        .then_inc(squares_made, 1)
                    pool.wait_ge(squares_hi, at(s, h, 2))
                    pool.tensor_tensor(p_lo[:, n % PT_RING, :], squares[:, cols],
                                       p_hi[:, n % PT_RING, :].bitcast(F32), ALU.subtract)\
                        .then_inc(squares_split, 1)

                for s in HEAD:
                    if s[0] == "start":
                        start()
                    elif s[0] == "weights":
                        split_lo(s[1] % 2, h * (2 * NT) + 2 * (PRE_TILES + s[1]))
                    elif s[0] == "b_combine":
                        b_combine(s[1])
                    elif s[0] == "m_norm":
                        m_norm(s[1])
                    elif s[0] == "a_norm":
                        a_norm(s[1])
                    elif s[0] == "b_squares":
                        b_squares(s[1])

            def mix_lo_part(par, js, n):
                pool.wait_ge(mix_hi_done, n + 1)
                pool.tensor_tensor(mix_lo[par][:, js, :], mix_raw[par][:, js, :], mix_hi[par][:, js, :].bitcast(F32),
                                   ALU.subtract).then_inc(mix_lo_done, 1)

            pool.wait_ge(pt_done, NMIX * HEADS)
            pool.wait_ge(t_full, PRE_T + NTB * HEADS)
            for par in range(2):
                mix_lo_part(par, slice(0, 3), par)
            for j in range(1, POOL_WO + 1):
                pool.wait_ge(wo_hi_done, j)
                pool.tensor_tensor(wo[j - 1][:, 1, :], wo_raw[j - 1][:, :], wo[j - 1][:, 0, :].bitcast(F32),
                                   ALU.subtract).then_inc(wo_lo_first, 1)
            mix_lo_part(1, slice(3, 9), 3)
            for par in range(2):
                mix_lo_part(par, slice(9, 12), 4 + par)
            with pool.Fori(0, ST // 2 - 1) as z:
                for par in range(2):
                    for p, js in enumerate((slice(0, 9), slice(9, 12))):
                        mix_lo_part(par, js, z * 4 + (6 + 2 * par + p))

        @block.vector
        def _(dve):
            steps = [0]

            def table(ins):
                steps[0] += 1
                ins.then_inc(table_step, 1)
                dve.wait_ge(table_step, steps[0])

            dve.wait_ge(gmem_full, 16)

            def normalise(raw, par, gain, r):
                one = slice(par, par + 1)
                dve.wait_ge(rows_sq, r + 1)
                dve.tensor_scalar(mean_sq[:, one], ssq[:, one], 1.0 / D, EPS, ALU.mult, ALU.add)\
                   .then_inc(mean_made, 1)
                dve.wait_ge(rows_std, r + 1)
                dve.reciprocal(rstd[:, one], std[:, one]).then_inc(rows_inv, 1)
                dve.wait_ge(mean_made, r + 1)
                dve.wait_ge(rows_inv, r * 4 + 1)
                dve.scalar_tensor_tensor(out=newton[:, one], in0=mean_sq[:, one], scalar=rstd[:, one],
                                         in1=rstd[:, one], op0=ALU.mult, op1=ALU.mult).then_inc(rows_inv, 1)
                dve.wait_ge(rows_inv, r * 4 + 2)
                dve.tensor_scalar(newton_by[:, one], newton[:, one], -0.5, 1.5, ALU.mult, ALU.add)\
                   .then_inc(rows_inv, 1)
                dve.wait_ge(rows_inv, r * 4 + 3)
                dve.tensor_tensor(rstd_fine[:, one], rstd[:, one], newton_by[:, one], ALU.mult).then_inc(rows_inv, 1)
                dve.wait_ge(rows_inv, r * 4 + 4)
                dve.scalar_tensor_tensor(out=rows[par], in0=raw[par][:, 0:D], scalar=rstd_fine[:, one],
                                         in1=gain[:, :], op0=ALU.mult, op1=ALU.mult).then_inc(rows_done, 1)

            for par in range(2):
                normalise(mem_raw, par, g_mem_b, par)
            for par in range(2):
                for u in range(2):
                    dve.wait_ge(t_hi, 2 * par + u + 1)
                    out = slice(4 * u, 4 * u + 4), slice(par * P, (par + 1) * P)
                    dve.tensor_tensor(mem_lo[:, out[0], out[1]], trans[:, u, :].rearrange("p (k n) -> p k n", k=4),
                                      mem_hi[:, out[0], out[1]].bitcast(F32), ALU.subtract).then_inc(t_free, 1)
            dve.wait_ge(gnorm_full, 16)
            normalise(rows_raw, 0, g_norm_b, 2)

            def prologue_step(q, par, more=True):
                dve.wait_ge(acc_full, q * 2 + (par + 1))
                out = mk_raw[:, bass.ds(q, 1), :].rearrange("p a n -> p (a n)") if par == 0 else \
                    mv_t[:, bass.ds(q * MEM, MEM)]
                dve.tensor_copy(out, acc[:, par, 0:MEM]).then_inc(acc_free, 1)
                if more:
                    normalise(rows_raw, 1 - par, g_norm_b, q * 2 + (3 + par))
                for u in range(2):
                    dve.wait_ge(t_hi, q * 4 + (5 + 2 * par + u))
                    cols = bass.ds(q * 2 * P + par * P, P)
                    dve.tensor_tensor(x_lo[:, 4 * u:4 * u + 4, cols],
                                      trans[:, u, :].rearrange("p (k n) -> p k n", k=4),
                                      x_hi[:, 4 * u:4 * u + 4, cols].bitcast(F32), ALU.subtract)\
                       .then_inc(t_free, 1)

            with dve.Fori(0, 3) as q:
                for par in range(2):
                    prologue_step(q, par)
            prologue_step(3, 0)
            prologue_step(3, 1, more=False)
            dve.wait_ge(consts_full, 96)
            table(dve.tensor_tensor(lam_prod, lam_in[:, 0:4:2, :], lam_in[:, 1:4:2, :], ALU.mult))
            table(dve.reduce_sum(lam_sums, lam_prod, AX.X))
            for i in range(2):
                table(dve.tensor_copy(sinks.rearrange("p (t g i) -> p t g i", t=4, g=2)[:, :, :, i],
                                      sink_in.rearrange("p (g t) -> p t g", g=2)))
            for s in range(2):
                dve.wait_ge(acc_full, 9 + s)
                dve.tensor_copy(av_t[:, CHUNK + s * HALF:CHUNK + (s + 1) * HALF], acc[:, s, :]).then_inc(acc_free, 1)
            for v in range(2):
                dve.wait_ge(t_full, 21 + v)
                dve.tensor_copy(mv_raw[:, 2 * v:2 * v + 2, :, :].rearrange("p h a n -> p (h a n)"), trans[:, v, :])\
                   .then_inc(t_free, 1)
            dve.wait_ge(lam_exp, 1)
            table(dve.tensor_tensor(neg_lam, lam_exps[:, 1:2], lam_exps[:, 0:1], ALU.subtract))
            table(dve.tensor_scalar(neg_lam, neg_lam, -LAM_INIT, None, ALU.add))
            table(dve.tensor_scalar(subln, subln, 0.5 * (1.0 - LAM_INIT), None, ALU.mult))
            dve.memset(ones[:, :].bitcast(F32), 1.0).then_inc(table_step, 1)
            steps[0] += 1
            dve.wait_ge(const_made, 5)
            table(dve.tensor_scalar(a_bias[CHUNK:P, :, :, :], a_bias[CHUNK:P, :, :, :], float(CHUNK), None, ALU.add))
            for t in (b_bias[:, :], a_bias[:, :, :, :].rearrange("p g t n -> p (g t n)")):
                table(dve.scalar_tensor_tensor(out=t, in0=t, scalar=-1.0, in1=t, op0=ALU.mult, op1=ALU.min))
            table(dve.tensor_scalar(a_bias[:, 1, :, :], a_bias[:, 1, :, :], 2.0 ** -4, None, ALU.mult))
            masks = [b_bias[0:CHUNK, SEQ - P + CHUNK:SEQ + P], b_bias[CHUNK:P, SEQ:SEQ + P],
                     a_bias[0:CHUNK, :, 0, 0:CHUNK]]
            for m in masks:
                table(dve.memset(m, MASKED))
            for s in range(2):
                dve.wait_ge(acc_full, 11 + s)
                dve.tensor_copy(a_k[:, CHUNK + s * HALF:CHUNK + (s + 1) * HALF], acc[:, s, :]).then_inc(acc_free, 1)
            for v in range(4):
                dve.wait_ge(t_full, 23 + v)
                dve.tensor_copy(a_v[:, 4 * v:4 * v + 4, :].rearrange("p c n -> p (c n)"), trans[:, v % 2, :])\
                   .then_inc(t_free, 1)

            with dve.Fori(0, HEADS) as h:
                def start():
                    dve.wait_ge(s_free_dve, h * len(S_BY_DVE))
                    dve.tensor_scalar(b_bias[:, :], b_bias[:, :], 0.25, None, ALU.mult).then_inc(bias_made, 1)
                    dve.tensor_scalar(a_bias[:, :, :, :], a_bias[:, :, :, :], 0.5, None, ALU.mult)\
                       .then_inc(bias_made, 1)
                    dve.wait_ge(bias_made, h * 2 + 2)

                parts = {"bk": 4, "bq": 2, "bv": 0, "aq": 0, "ag": 1, "mq": 1, "mg": 1, "bg": 1}
                per_turn = 2 * sum(parts.values())
                before = {}
                n = 0
                for w, (name, _, _) in enumerate(TILES):
                    for s in range(2):
                        n += parts[name]
                        before[(w, s)] = n

                def evacuate(w, s):
                    name = TILES[w][0]
                    cols = slice(s * HALF, (s + 1) * HALF)
                    if name == "bv":
                        dve.wait_ge(b_gated, h * 2)
                    if parts[name]:
                        dve.wait_ge(acc_part, h * per_turn + before[(w, s)])
                    else:
                        dve.wait_ge(acc_full, at(2 * w + s, h, 2 * NT, PRE_ACC))
                    if name == "bk":
                        for c in range(2):
                            ps = slice(c * DK, (c + 1) * DK)
                            last = dve.tensor_tensor(k_lo[ps, cols], acc[ps, s, :], k_b[ps, c, cols].bitcast(F32),
                                                     ALU.subtract)
                    elif name == "bq":
                        for c in range(2):
                            ps = slice(c * DK, (c + 1) * DK)
                            po = slice((1 - c) * DK, (2 - c) * DK)
                            last = dve.scalar_tensor_tensor(out=q_b[po, c, cols], in0=acc[ps, s, :], scalar=QK_SCALE,
                                                            in1=q_b[ps, c, cols].bitcast(F32), op0=ALU.mult,
                                                            op1=ALU.subtract)
                    elif name == "bv":
                        last = dve.tensor_copy(bv_t[:, cols], acc[:, s, :])
                    elif name == "aq":
                        last = dve.tensor_scalar(a_q[:, cols], acc[:, s, :], QK_SCALE, None, ALU.mult)
                    elif name == "mq":
                        last = dve.tensor_tensor(q_m_lo[:, cols], acc[:, s, :], q_m_hi[:, cols].bitcast(F32),
                                                 ALU.subtract)
                    else:
                        g = gates[name[0]]
                        last = dve.scalar_tensor_tensor(out=g[:, cols], in0=g[:, cols], scalar=1.0,
                                                        in1=acc[:, s, :], op0=ALU.add, op1=ALU.mult)
                    last.then_inc(acc_free, 1)

                def b_scores(i, p):
                    if p == 0 and i >= 2:
                        g = i // 2 - 1
                        dve.wait_ge(t_full, at(T_AT[("b_spread", g, g)], h, NTB, PRE_T))
                    elif p == 0:
                        dve.wait_ge(t_full, h * NTB + PRE_T)
                        dve.wait_ge(b_normed, h * 2)
                    if p == 0 and i >= 1:
                        dve.wait_ge(b_neg_made, at(i - 1, h, ST))
                    pieces = b_pieces(i)
                    a, n = pieces[p]
                    for c in range(2):
                        unit = S_AT[("b", i, p, c)]
                        dve.wait_ge(s_full, at(unit, h, NS))
                        dve.nop(nofuse=True)
                        rel = SEQ - P - i * P + a
                        dve.tensor_tensor_reduce(out=logits[:, i % 2, c, a:a + n],
                                                 in0=score[:, unit % S_RING, 0:n], in1=b_bias[:, rel:rel + n],
                                                 scale=1.0, scalar=-3e38, op0=ALU.add, op1=ALU.max,
                                                 accum_out=b_max[:, 2 * c + p:2 * c + p + 1])\
                           .then_inc(s_free_dve, 1)
                    if p < len(pieces) - 1:
                        return
                    dve.wait_ge(s_free_dve, at(S_BY_DVE[("b", i, p, 1)], h, len(S_BY_DVE)))
                    dve.tensor_reduce(b_neg[:, 2 * (i % 2):2 * (i % 2) + 2],
                                      b_max.rearrange("p (c n) -> p c n", c=2)[:, :, 0:len(pieces)],
                                      axis=AX.X, op=ALU.max, negate=True).then_inc(b_neg_made, 1)

                def b_combine(i):
                    width = sum(n for _, n in b_pieces(i))
                    k = 2 * (i % 2)
                    dve.wait_ge(b_exp, at(2 * i + 1, h, 2 * ST))
                    dve.reciprocal(b_inv[:, k:k + 2], b_sum[:, k:k + 2]).then_inc(b_inv_made, 1)
                    dve.wait_ge(b_inv_made, at(i, h, ST))
                    dve.wait_ge(b_scaled, at(i, h, ST))
                    dve.scalar_tensor_tensor(out=logits[:, i % 2, 0, 0:width], in0=logits[:, i % 2, 0, 0:width],
                                             scalar=b_inv[:, k:k + 1], in1=logits[:, i % 2, 1, 0:width],
                                             op0=ALU.mult, op1=ALU.add).then_inc(b_ready, 1)

                def take_lo(step, out, hi):
                    dve.wait_ge(t_hi, at(T_SPLIT[step], h, len(T_SPLIT), 20))
                    dve.tensor_tensor(out, trans[:, T_AT[step] % T_RING, :], hi.bitcast(F32), ALU.subtract)\
                       .then_inc(t_free, 1)

                def gate(g, m):
                    cols = slice(m * MEM, (m + 1) * MEM)
                    if g == "a":
                        dve.wait_ge(a_mixed, at(m, h, 4))
                    else:
                        dve.wait_ge(pt_done, at(PT_MIX[("m_spread", m)], h, NMIX))
                    w = [n for n, _, _ in TILES].index(f"{g}g")
                    dve.wait_ge(acc_free, at(2 * w + m // 2, h, 2 * NT, PRE_ACC))
                    dve.scalar_tensor_tensor(out=gates[g][:, cols], in0=mixo[:, 0:MEM], scalar=0.5,
                                             in1=gates[g][:, cols], op0=ALU.mult, op1=ALU.mult)\
                       .then_inc(o_free, 1)

                def b_take(g):
                    if g == 0:
                        dve.wait_ge(t_full, at(T_AT[("v_spread", 1)], h, NTB, PRE_T))
                    dve.wait_ge(pt_done, at(PT_MIX[("b_spread", g, g)], h, NMIX))
                    dve.tensor_copy(b_out[:, g * MEM:(g + 1) * MEM], mixo[:, 0:MEM]).then_inc(o_free, 1)

                def m_scores(m):
                    unit = S_AT[("m", m)]
                    dve.wait_ge(s_full, at(unit, h, NS))
                    dve.tensor_reduce(m_max, score[:, unit % S_RING, :].rearrange("p (a n) -> p a n", a=2),
                                      axis=AX.X, op=ALU.max).then_inc(m_max_made, 1)
                    dve.wait_ge(m_max_made, at(m, h, 4))
                    dve.wait_ge(m_ready, at(m - 1, h, 4) if m else h * 4)
                    dve.tensor_scalar(m_neg, m_max, -M_SCALE, None, ALU.mult).then_inc(m_neg_made, 1)

                def m_norm(m):
                    dve.wait_ge(s_free_act, at(m, h, 4))
                    dve.reciprocal(m_inv, m_sum).then_inc(m_inv_made, 1)

                def a_scores(m):
                    dve.wait_ge(a_ready, at(m - 1, h, 4) if m else h * 4)
                    for g in range(2):
                        unit = S_AT[("a", m, g)]
                        dve.wait_ge(s_full, at(unit, h, NS))
                        s = score[:, unit % S_RING, :].rearrange("p (i n) -> p i n", i=2)
                        for c in range(2):
                            ps = slice(c * CHUNK, (c + 1) * CHUNK)
                            bias = a_bias[ps, g, 0:2, :] if m == 0 else \
                                a_bias[ps, g, 1:2, :].broadcast_to([CHUNK, 2, P])
                            last = dve.tensor_tensor(a_band[ps, 2 * g:2 * g + 2, :], s[ps, :, c * CHUNK:c * CHUNK + P],
                                                     bias, ALU.add)
                        last.then_inc(s_free_dve, 1)
                    dve.wait_ge(s_free_dve, at(S_BY_DVE[("a", m, 1)], h, len(S_BY_DVE)))
                    dve.reduce_max(a_max, a_band[:, :, :], AX.X).then_inc(a_max_made, 1)
                    dve.wait_ge(a_max_made, at(m, h, 4))
                    sink = sinks[:, bass.ds(h * 4, 4)]
                    dve.tensor_tensor(a_top, a_max, sink, ALU.max).then_inc(a_top_made, 1)
                    dve.wait_ge(a_top_made, at(m, h, 4))
                    dve.tensor_scalar(a_neg, a_top, -1.0, None, ALU.mult).then_inc(a_neg_made, 1)
                    dve.wait_ge(a_neg_made, at(m, h, 4))
                    dve.tensor_tensor(a_off, sink, a_neg, ALU.add).then_inc(a_off_made, 1)

                def a_norm(m):
                    dve.wait_ge(a_exp_made, at(m, h, 4))
                    dve.tensor_tensor(a_den, a_sum, a_exp, ALU.add).then_inc(a_den_made, 1)
                    dve.wait_ge(a_den_made, at(m, h, 4))
                    dve.reciprocal(a_inv, a_den).then_inc(a_inv_made, 1)

                def a_spread(m):
                    step = ("a_spread", m)
                    dve.wait_ge(t_full, at(T_AT[step], h, NTB, PRE_T))
                    dve.wait_ge(a_mixed, at(m - 1, h, 4) if m else h * 4)
                    dve.tensor_copy(a_pt[:, :, :].rearrange("p a n -> p (a n)"), trans[:, T_AT[step] % T_RING, :])\
                       .then_inc(t_free, 1)

                def b_squares(s):
                    cols = slice(s * HALF, (s + 1) * HALF)
                    step = ("b_squares", s)
                    dve.wait_ge(t_full, at(T_AT[step], h, NTB, PRE_T))
                    dve.tensor_scalar(inv_rms[:, cols], trans[:, T_AT[step] % T_RING, :], 1.0 / P, EPS,
                                      ALU.mult, ALU.add).then_inc(t_free, 1)

                def b_finish(s):
                    cols = slice(s * HALF, (s + 1) * HALF)
                    dve.wait_ge(rms_made, at(s, h, 2))
                    dve.reciprocal(inv_rms[:, cols], inv_rms[:, cols]).then_inc(inv_made, 1)
                    dve.wait_ge(inv_made, at(s, h, 2))
                    dve.tensor_tensor(b_out[:, cols], b_out[:, cols], inv_rms[:, cols], ALU.mult)\
                       .then_inc(b_normed, 1)

                def b_gate():
                    for s in range(2):
                        cols = slice(s * HALF, (s + 1) * HALF)
                        dve.wait_ge(b_normed, at(s, h, 2))
                        dve.wait_ge(acc_free, at(2 * (NT - 1) + s, h, 2 * NT, PRE_ACC))
                        dve.scalar_tensor_tensor(out=gates["b"][:, cols], in0=b_out[:, cols], scalar=subln,
                                                 in1=gates["b"][:, cols], op0=ALU.mult, op1=ALU.mult)\
                           .then_inc(b_gated, 1)

                for s in HEAD:
                    if s[0] == "start":
                        start()
                    elif s[0] == "evacuate":
                        evacuate(*s[1:])
                    elif s[0] == "b_scores":
                        b_scores(*s[1:])
                    elif s[0] == "b_combine":
                        b_combine(s[1])
                    elif s[0] == "v_spread":
                        half = s[1]
                        take_lo(s, v_lo[:, 4 * half:4 * half + 4, :].rearrange("p j n -> p (j n)"),
                                v_hi[:, 4 * half:4 * half + 4, :].rearrange("p j n -> p (j n)"))
                    elif s[0] in ("b_spread", "m_spread"):
                        slot = PT_AT[s] % PT_RING
                        take_lo(s, p_lo[:, slot, :], p_hi[:, slot, :])
                    elif s[0] == "b_mix":
                        if s[1] == s[2]:
                            b_take(s[1])
                    elif s[0] in ("m_mix", "a_mix"):
                        gate(s[0][0], s[1])
                    elif s[0] == "m_scores":
                        m_scores(s[1])
                    elif s[0] == "m_norm":
                        m_norm(s[1])
                    elif s[0] == "a_scores":
                        a_scores(s[1])
                    elif s[0] == "a_norm":
                        a_norm(s[1])
                    elif s[0] == "a_spread":
                        a_spread(s[1])
                    elif s[0] == "b_squares":
                        b_squares(s[1])
                    elif s[0] == "b_finish":
                        b_finish(s[1])
                    elif s[0] == "b_gate":
                        b_gate()

            dve.wait_ge(mix_hi_done, 3)
            dve.wait_ge(pt_done, NMIX * HEADS)
            dve.wait_ge(t_full, PRE_T + NTB * HEADS)
            dve.tensor_tensor(mix_lo[0][:, 3:9, :], mix_raw[0][:, 3:9, :], mix_hi[0][:, 3:9, :].bitcast(F32),
                              ALU.subtract).then_inc(mix_lo_mid, 1)
            for j in range(POOL_WO + 1, MIX_TILES):
                dve.wait_ge(wo_hi_done, j)
                dve.tensor_tensor(wo[j - 1][:, 1, :], wo_raw[j - 1][:, :],
                                  wo[j - 1][:, 0, :].bitcast(F32), ALU.subtract).then_inc(wo_lo_done, 1)

            def finish(par, z):
                dve.wait_ge(res_full[par], z * 16 + 16)
                dve.wait_ge(stored[par], z * 32)
                for s in range(2):
                    cols = slice(s * HALF, (s + 1) * HALF)
                    dve.wait_ge(y_full, z * 4 + (2 * par + s + 1))
                    dve.tensor_tensor(y_row[:, par, cols], y_acc[2 * par + s], x_res[:, par, cols], ALU.add)\
                       .then_inc(y_added[par], 1)
                dve.wait_ge(y_sqd, z * 4 + (2 * par + 2))
                dve.tensor_tensor(ssq[:, par:par + 1], y_ssq[:, 2 * par:2 * par + 1], y_ssq[:, 2 * par + 1:2 * par + 2],
                                  ALU.add).then_inc(y_sum, 1)
                dve.wait_ge(y_std, z * 2 + (par + 1))
                dve.reciprocal(rstd[:, par:par + 1], std[:, par:par + 1]).then_inc(y_inv, 1)
                dve.wait_ge(y_inv, z * 2 + (par + 1))
                for s in range(2):
                    cols = slice(s * HALF, (s + 1) * HALF)
                    dve.scalar_tensor_tensor(out=y_row[:, par, cols], in0=y_row[:, par, cols],
                                             scalar=rstd[:, par:par + 1], in1=g_fin[:, cols],
                                             op0=ALU.mult, op1=ALU.mult).then_inc(y_done, 1)

            dve.wait_ge(gfin_full, 16)
            with dve.Fori(0, ST // 2) as z:
                for par in range(2):
                    finish(par, z)

        @block.tensor
        def _(pe):
            def product(out, a_hi, a_lo, b_hi, b_lo, start, stop):
                pe.matmul(out, a_hi, b_hi, start=start, stop=False, skip_group_check=True)
                pe.matmul(out, a_hi, b_lo, start=False, stop=False, skip_group_check=True)
                return pe.matmul(out, a_lo, b_hi, start=False, stop=stop, skip_group_check=True)

            def spread_rows(par, u):
                for k in range(4):
                    cols = slice((4 * u + k) * P, (4 * u + k + 1) * P)
                    last = pe.transpose(trans[:, u, k * P:(k + 1) * P], rows[par][:, cols], ident[:, :])
                last.then_inc(t_full, 1)

            def keep_busy(n):
                for _ in range(n):
                    pe.transpose(score[:, 0, 0:P], ident[:, :], ident[:, :])

            pe.wait_ge(const_made, 2)
            keep_busy(BUSY[0])
            for par in range(2):
                if par == 1:
                    keep_busy(BUSY[1])
                pe.wait_ge(rows_done, par + 1)
                for u in range(2):
                    if par:
                        pe.wait_ge(t_free, u + 1)
                    spread_rows(par, u)
            keep_busy(BUSY[2])
            pe.wait_ge(t_free, 4)
            with pe.Fori(0, 4) as q:
                for par in range(2):
                    pe.wait_ge(w_lo_done, q * 2 + (par + 1))
                    pe.wait_ge(acc_free, q * 2)
                    for k in range(KT):
                        w = slice(k * P, (k + 1) * P)
                        last = product(acc[:, par, 0:MEM], w_hi[:, par, w], w_lo[:, par, w], mem_hi[:, k, :],
                                       mem_lo[:, k, :], k == 0, k == KT - 1)
                    last.then_inc(acc_full, 1)
                    pe.wait_ge(rows_done, q * 2 + (par + 3))
                    for u in range(2):
                        pe.wait_ge(t_free, q * 4 + (2 * par + u + 3))
                        spread_rows(par, u)

            def project(w, s, k):
                tile = slice(k * P, (k + 1) * P)
                cols = slice(s * HALF, (s + 1) * HALF)
                return product(acc[:, s, :], w_hi[:, w % 2, tile], w_lo[:, w % 2, tile], x_hi[:, k, cols],
                               x_lo[:, k, cols], k == 0, k == KT - 1)

            for n in (8, 9):
                pe.wait_ge(w_lo_done, n + 1)
                for s in range(2):
                    unit = 8 + 2 * (n - 8) + s
                    pe.wait_ge(acc_free, unit - 1)
                    pe.wait_ge(t_free, 12 + 8 * s)
                    for k in range(KT):
                        last = project(n, s, k)
                    last.then_inc(acc_full, 1)
                if n == 8:
                    for v in range(2):
                        pe.wait_ge(t_free, 19 + v)
                        for b in range(4):
                            last = pe.transpose(trans[:, v, b * P:(b + 1) * P],
                                                mv_t[:, (4 * v + b) * P:(4 * v + b + 1) * P], ident[:, :])
                        last.then_inc(t_full, 1)
            pe.wait_ge(const_made, 6)
            pe.wait_ge(acc_free, 10)
            for v in range(4):
                pe.wait_ge(t_free, 21 + v)
                for b in range(4):
                    c = 4 * v + b
                    last = pe.transpose(trans[:, v % 2, b * P:(b + 1) * P], av_t[:, c * CHUNK:c * CHUNK + P],
                                        ident[:, :])
                last.then_inc(t_full, 1)

            with pe.Fori(0, HEADS) as h:
                def s_bank(key):
                    n = S_AT[key]
                    if n < S_RING:
                        pe.wait_ge(s_free_dve, h * len(S_BY_DVE))
                        pe.wait_ge(s_free_act, h * len(S_BY_ACT))
                    else:
                        last = S_UNITS[n - S_RING]
                        if last in S_BY_DVE:
                            pe.wait_ge(s_free_dve, at(S_BY_DVE[last], h, len(S_BY_DVE)))
                        else:
                            pe.wait_ge(s_free_act, at(S_BY_ACT[last], h, len(S_BY_ACT)))
                    return score[:, n % S_RING, :]

                def t_bank(step):
                    n = T_AT[step]
                    pe.wait_ge(t_free, at(n - T_RING, h, NTB, PRE_T))
                    return trans[:, n % T_RING, :]

                def o_bank(key):
                    n = O_AT[key]
                    pe.wait_ge(o_free, at(n - 1, h, NO) if n else h * NO)
                    return mixo[:, 0:MEM]

                def project_quarter(w, s, q):
                    if q == 0:
                        if s == 0:
                            pe.wait_ge(w_lo_done, at(w, h, NT, PRE_TILES))
                        pe.wait_ge(acc_free, at(2 * w + s - 2, h, 2 * NT, PRE_ACC))
                    for k in (2 * q, 2 * q + 1):
                        last = project(w, s, k)
                    if q == 3:
                        last.then_inc(acc_full, 1)

                def b_scores(i, p):
                    if i == 0:
                        pe.wait_ge(acc_free, at(3, h, 2 * NT, PRE_ACC))
                    rows_i = slice(i * P, (i + 1) * P)
                    a, n = b_pieces(i)[p]
                    for c in range(2):
                        out = s_bank(("b", i, p, c))[:, 0:n]
                        ps = slice(c * DK, (c + 1) * DK)
                        pe.matmul(out, q_b[:, c, rows_i], k_b[:, c, a:a + n], start=True, stop=False,
                                  skip_group_check=True)
                        pe.matmul(out, q_b[ps, c, rows_i], k_lo[ps, a:a + n], start=False, stop=True,
                                  skip_group_check=True).then_inc(s_full, 1)

                def v_spread(half):
                    if half == 0:
                        pe.wait_ge(acc_free, at(5, h, 2 * NT, PRE_ACC))
                    out = t_bank(("v_spread", half))
                    for j in range(4):
                        cols = slice((4 * half + j) * P, (4 * half + j + 1) * P)
                        last = pe.transpose(out[:, j * P:(j + 1) * P], bv_t[:, cols], ident[:, :])
                    last.then_inc(t_full, 1)

                def b_spread(g, u):
                    if u == 0:
                        pe.wait_ge(b_ready, at(2 * g + 1, h, ST))
                    out = t_bank(("b_spread", g, u))
                    for j in range(2):
                        for i in range(2):
                            last = pe.transpose(out[:, (2 * j + i) * P:(2 * j + i + 1) * P],
                                                logits[:, i, 0, (2 * u + j) * P:(2 * u + j + 1) * P], ident[:, :])
                    last.then_inc(t_full, 1)

                def p_slot(step):
                    pe.wait_ge(t_free, at(T_AT[step], h, NTB, PRE_T))
                    return PT_AT[step] % PT_RING

                def b_mix(g, u):
                    if g == 0:
                        pe.wait_ge(t_free, at(T_AT[("v_spread", 1)], h, NTB, PRE_T))
                    out = o_bank(("b_mix", g)) if u == 0 else mixo[:, 0:MEM]
                    slot = p_slot(("b_spread", g, u))
                    for j in range(2):
                        cols = slice(j * MEM, (j + 1) * MEM)
                        last = product(out, v_hi[:, 2 * u + j, :], v_lo[:, 2 * u + j, :], p_hi[:, slot, cols],
                                       p_lo[:, slot, cols], u == 0 and j == 0, u == g and j == 1)
                    last.then_inc(pt_done, 1)

                def m_scores(m):
                    if m == 0:
                        pe.wait_ge(acc_free, at(11, h, 2 * NT, PRE_ACC))
                        pe.wait_ge(mkv_lo, h * 2 + 2)
                    out = s_bank(("m", m))
                    for i in range(2):
                        r = slice((2 * m + i) * P, (2 * m + i + 1) * P)
                        last = product(out[:, i * MEM:(i + 1) * MEM], q_m_hi[:, r], q_m_lo[:, r], mk_hi[:, :],
                                       mk_lo[:, :], True, True)
                    last.then_inc(s_full, 1)

                def m_spread(m):
                    pe.wait_ge(m_ready, at(m, h, 4))
                    out = t_bank(("m_spread", m))
                    for j in range(2):
                        for i in range(2):
                            last = pe.transpose(out[:, (2 * j + i) * P:(2 * j + i + 1) * P],
                                                m_probs[:, i, j * P:(j + 1) * P], ident[:, :])
                    last.then_inc(t_full, 1)

                def m_mix(m):
                    out = o_bank(("m_mix", m))
                    slot = p_slot(("m_spread", m))
                    for j in range(2):
                        cols = slice(j * MEM, (j + 1) * MEM)
                        last = product(out, mv_hi[:, j, :], mv_lo[:, j, :], p_hi[:, slot, cols],
                                       p_lo[:, slot, cols], j == 0, j == 1)
                    last.then_inc(pt_done, 1)

                def a_scores(m):
                    if m == 0:
                        pe.wait_ge(acc_free, at(7, h, 2 * NT, PRE_ACC))
                    outs = [s_bank(("a", m, g)) for g in range(2)]
                    for i in range(2):
                        t = 2 * m + i
                        for g in range(2):
                            ps = slice(g * DK, (g + 1) * DK)
                            last = pe.matmul(outs[g][:, i * MEM:i * MEM + 3 * CHUNK], a_q[ps, t * P:(t + 1) * P],
                                             a_k[ps, t * P:t * P + 3 * CHUNK], start=True, stop=True,
                                             skip_group_check=True)
                            if i == 1:
                                last.then_inc(s_full, 1)

                def a_spread(m):
                    pe.wait_ge(a_ready, at(m, h, 4))
                    out = t_bank(("a_spread", m))
                    for n in range(4):
                        last = pe.transpose(out[:, n * P:(n + 1) * P], a_probs[:, n, :], ident[:, :])
                    last.then_inc(t_full, 1)

                def a_mix(m):
                    out = o_bank(("a_mix", m))
                    pe.wait_ge(t_free, at(T_AT[("a_spread", m)], h, NTB, PRE_T))
                    for i in range(2):
                        for c in range(2):
                            chunk = 2 * (2 * m + i) + c
                            for g in range(2):
                                ps = slice(g * DK, (g + 1) * DK)
                                last = pe.matmul(out[ps, i * P + c * CHUNK:i * P + (c + 1) * CHUNK], a_v[:, chunk, ps],
                                                 a_pt[:, 2 * g + i, c * CHUNK:(c + 1) * CHUNK], start=True, stop=True,
                                                 skip_group_check=True)
                    last.then_inc(a_mixed, 1)

                def b_squares(s):
                    out = t_bank(("b_squares", s))
                    slot = PT_AT[("b_squares", s)] % PT_RING
                    pe.wait_ge(squares_split, at(s, h, 2))
                    pe.matmul(out, ones[:, :], p_hi[:, slot, :], start=True, stop=False, skip_group_check=True)
                    pe.matmul(out, ones[:, :], p_lo[:, slot, :], start=False, stop=True, skip_group_check=True)\
                      .then_inc(t_full, 1)

                for s in HEAD:
                    if s[0] == "project":
                        project_quarter(*s[1:])
                    elif s[0] == "b_scores":
                        b_scores(*s[1:])
                    elif s[0] == "v_spread":
                        v_spread(s[1])
                    elif s[0] == "b_spread":
                        b_spread(*s[1:])
                    elif s[0] == "b_mix":
                        b_mix(*s[1:])
                    elif s[0] == "m_scores":
                        m_scores(s[1])
                    elif s[0] == "m_spread":
                        m_spread(s[1])
                    elif s[0] == "m_mix":
                        m_mix(s[1])
                    elif s[0] == "a_scores":
                        a_scores(s[1])
                    elif s[0] == "a_spread":
                        a_spread(s[1])
                    elif s[0] == "a_mix":
                        a_mix(s[1])
                    elif s[0] == "b_squares":
                        b_squares(s[1])

            w_out_hi = [w_hi[:, 0, :]] + [t[:, 0, :] for t in wo]
            w_out_lo = [w_lo[:, 0, :]] + [t[:, 1, :] for t in wo]

            def y_product(par, s, j):
                cols = slice(s * HALF, (s + 1) * HALF)
                return product(y_acc[2 * par + s], mix_hi[par][:, j, :], mix_lo[par][:, j, :], w_out_hi[j][:, cols],
                               w_out_lo[j][:, cols], j == 0, j == MIX_TILES - 1)

            def w_out_ready(j):
                if j == 0:
                    pe.wait_ge(w_lo_done, PRE_TILES + NT * HEADS + 1)
                elif j <= POOL_WO:
                    pe.wait_ge(wo_lo_first, j)
                else:
                    pe.wait_ge(wo_lo_done, j - POOL_WO)

            pe.wait_ge(t_free, PRE_T + NTB * HEADS)
            pe.wait_ge(s_free_dve, len(S_BY_DVE) * HEADS)
            pe.wait_ge(s_free_act, len(S_BY_ACT) * HEADS)
            for j in range(7):
                w_out_ready(j)
                for par in range(2):
                    if j == 0:
                        pe.wait_ge(mix_lo_done, 1 + par)
                    if j == 3:
                        pe.wait_ge(*((mix_lo_done, 3) if par else (mix_lo_mid, 1)))
                    for s in range(2):
                        y_product(par, s, j)
            for par in range(2):
                pe.wait_ge(mix_lo_done, 4 + par)
                for s in range(2):
                    for j in range(7, MIX_TILES):
                        w_out_ready(j)
                        last = y_product(par, s, j)
                    last.then_inc(y_full, 1)
            with pe.Fori(0, ST // 2 - 1) as z:
                for par in range(2):
                    pe.wait_ge(mix_lo_done, z * 4 + (7 + 2 * par))
                    for s in range(2):
                        pe.wait_ge(y_added[par], z * 2 + (s + 1))
                        for j in range(MIX_TILES):
                            last = y_product(par, s, j)
                        last.then_inc(y_full, 1)


_INS = ["x", "mem", "w_in", "g_norm", "a_sinks", "b_lambda_q1", "b_lambda_k1", "b_lambda_q2", "b_lambda_k2",
        "b_subln_g", "g_mem", "w_mem_kv", "w_out", "g_final"]


def kernel(**inputs):
    import numpy as np
    import concourse.bacc as bacc
    from concourse.bass_utils import run_bass_kernel_spmd

    nc = bacc.Bacc("TRN2", target_bir_lowering=False, num_devices=1)
    arrays, args = {}, []
    for name in _INS:
        a = np.ascontiguousarray(inputs[name])
        arrays[f"in_{name}"] = a
        args.append(nc.dram_tensor(f"in_{name}", a.shape, mybir.dt.from_np(a.dtype), kind="ExternalInput").ap())
    args.append(nc.dram_tensor("out_y", (1, SEQ, D), F32, kind="ExternalOutput").ap())
    build(nc, *args)
    r = run_bass_kernel_spmd(nc, [arrays], core_ids=[0])
    return r.results[0]["out_y"]
```
